# Optimizing a Trainium2 kernel written in Bass

```python
import jax
import jax.numpy as jnp
from jax import lax
import numpy as np
import math
import jax, jax.numpy as jnp

D_MODEL = 1024
BATCH = 1
SEQ = 256
DEPTH = 1

NORM_EPS = 1e-6
D_FF = 2816

ATTN_HEAD_DIM = 64
ATTN_HEADS_PER_GROUP = 4
ATTN_GROUPS = ((128, 1), (512, 4), (2048, 16))
N_ATTN_GROUPS = 3
ATTN_WIDTH = N_ATTN_GROUPS * ATTN_HEADS_PER_GROUP * ATTN_HEAD_DIM
ATTN_OUT_WIDTH = ATTN_HEADS_PER_GROUP * ATTN_HEAD_DIM
ROPE_THETA = 500000.0
ROPE_DIM = ATTN_HEAD_DIM // 4

RWKV_HEAD_DIM = 64
RWKV_WIDTH = D_MODEL
RWKV_HEADS = RWKV_WIDTH // RWKV_HEAD_DIM
DECAY_LORA = 64
ICLR_LORA = 64
GATE_LORA = 160
RWKV_GN_EPS = 64e-5
RWKV_STREAM = 3 * RWKV_WIDTH + DECAY_LORA + ICLR_LORA + GATE_LORA

IN_COLS = 3 * ATTN_WIDTH + RWKV_STREAM + 2 * D_MODEL


def rms_norm(x, gain):
    xf = x.astype(jnp.float32)
    y = xf * lax.rsqrt(jnp.mean(xf * xf, axis=-1, keepdims=True) + NORM_EPS)
    return (y * gain.astype(jnp.float32)).astype(x.dtype)

def swiglu(h, w_gate, w_up, w_down):
    return (jax.nn.silu(h @ w_gate) * (h @ w_up)) @ w_down

def partial_rope(x, positions):
    half = ROPE_DIM // 2
    inv_freq = jnp.power(ROPE_THETA, -jnp.arange(half, dtype=jnp.float32) * (2.0 / ROPE_DIM))
    ang = positions.astype(jnp.float32)[:, None] * inv_freq[None, :]
    cos = jnp.cos(ang)[None, :, None, :]
    sin = jnp.sin(ang)[None, :, None, :]
    xr = x[..., :ROPE_DIM].astype(jnp.float32)
    x1, x2 = xr[..., :half], xr[..., half:]
    rot = jnp.concatenate([x1 * cos - x2 * sin, x2 * cos + x1 * sin], axis=-1).astype(x.dtype)
    return jnp.concatenate([rot, x[..., ROPE_DIM:]], axis=-1)

def dilated_group(q, k, v, window, dilation):
    B, S, H, Dh = q.shape
    n = window // dilation
    L = S // dilation
    nb = -(-L // n)
    Lp = nb * n

    def to_sub(t):
        t = t.reshape(B, L, dilation, H, Dh).transpose(0, 2, 3, 1, 4)
        t = jnp.pad(t, ((0, 0), (0, 0), (0, 0), (0, Lp - L), (0, 0)))
        return t.reshape(B, dilation, H, nb, n, Dh)

    def with_prev(t):
        prev = jnp.pad(t, ((0, 0), (0, 0), (0, 0), (1, 0), (0, 0), (0, 0)))[:, :, :, :-1]
        return jnp.concatenate([prev, t], axis=4)

    def from_sub(t):
        t = t.reshape(B, dilation, H, Lp, t.shape[-1])[:, :, :, :L]
        return t.transpose(0, 3, 1, 2, 4).reshape(B, S, H, t.shape[-1])

    qb = to_sub(q)
    kw = with_prev(to_sub(k))
    vw = with_prev(to_sub(v))
    s = jnp.einsum('brhiqd,brhikd->brhiqk', qb, kw, preferred_element_type=jnp.float32)
    qi = jnp.arange(n)[:, None]
    ki = jnp.arange(2 * n)[None, :]
    rel = qi + n - ki
    band = (rel >= 0) & (rel <= n)
    blk = jnp.arange(nb)[:, None, None]
    valid = band[None] & ((blk > 0) | (ki[None] >= n))
    s = jnp.where(valid, s, -jnp.inf)
    m = jnp.max(s, axis=-1)
    p = jnp.exp(s - m[..., None])
    l = jnp.sum(p, axis=-1)
    acc = jnp.einsum('brhiqk,brhikd->brhiqd', p, vw.astype(jnp.float32))
    return from_sub(acc), from_sub(m[..., None])[..., 0], from_sub(l[..., None])[..., 0]

def dilated_attention(qkv, positions):
    B, S, _ = qkv.shape
    G, Hg, Dh = N_ATTN_GROUPS, ATTN_HEADS_PER_GROUP, ATTN_HEAD_DIM
    q, k, v = jnp.split(qkv, 3, axis=-1)
    q = partial_rope(q.reshape(B, S, G * Hg, Dh), positions) * (Dh ** -0.5)
    k = partial_rope(k.reshape(B, S, G * Hg, Dh), positions)
    v = v.reshape(B, S, G * Hg, Dh)
    accs, ms, ls = [], [], []
    for g, (window, dilation) in enumerate(ATTN_GROUPS):
        sl = slice(g * Hg, (g + 1) * Hg)
        acc, m, l = dilated_group(q[:, :, sl], k[:, :, sl], v[:, :, sl], window, dilation)
        accs.append(acc)
        ms.append(m)
        ls.append(l)
    m_all = jnp.stack(ms)
    c = jnp.exp(m_all - jnp.max(m_all, axis=0))
    num = jnp.sum(c[..., None] * jnp.stack(accs), axis=0)
    den = jnp.sum(c * jnp.stack(ls), axis=0)
    out = (num / den[..., None]).astype(qkv.dtype)
    return out.reshape(B, S, Hg * Dh)

def token_shift(z, mu):
    prev = jnp.pad(z, ((0, 0), (1, 0), (0, 0)))[:, :-1]
    return z + (prev - z) * mu

def wkv7_scan(r, w, k, v, a, b):
    B, S, H, N = r.shape

    def step(state, inp):
        r_t, w_t, k_t, v_t, a_t, b_t = inp
        sa = jnp.einsum('bhvk,bhk->bhv', state, a_t)
        state = (state * w_t[:, :, None, :] + sa[..., None] * b_t[:, :, None, :]
                 + v_t[..., None] * k_t[:, :, None, :])
        return state, jnp.einsum('bhvk,bhk->bhv', state, r_t)

    xs = tuple(jnp.moveaxis(t.astype(jnp.float32), 1, 0) for t in (r, w, k, v, a, b))
    _, ys = lax.scan(step, jnp.zeros((B, H, N, N), jnp.float32), xs)
    return jnp.moveaxis(ys, 0, 1)

def rwkv7_time_mix(z, w0, w2, a0, a2, g2, k_k, k_a, r_k, ln_w, ln_b, w_out):
    B, S, _ = z.shape
    RW, H, N = RWKV_WIDTH, RWKV_HEADS, RWKV_HEAD_DIM
    o1, o2, o3 = RW, 2 * RW, 3 * RW
    o4, o5 = o3 + DECAY_LORA, o3 + DECAY_LORA + ICLR_LORA
    r, k, v = z[..., :o1], z[..., o1:o2], z[..., o2:o3]
    zw, za, zg = z[..., o3:o4], z[..., o4:o5], z[..., o5:]
    logw = -jax.nn.softplus(-(w0 + jnp.tanh(zw) @ w2)) - 0.5
    decay = jnp.exp(-jnp.exp(logw.astype(jnp.float32)))
    a = jax.nn.sigmoid(a0 + za @ a2)
    g = jax.nn.sigmoid(zg) @ g2
    kk = (k * k_k).astype(jnp.float32).reshape(B, S, H, N)
    kk = kk / jnp.maximum(jnp.sqrt(jnp.sum(kk * kk, axis=-1, keepdims=True)), 1e-12)
    k = k * (1.0 + (a - 1.0) * k_a)
    rh = r.reshape(B, S, H, N).astype(jnp.float32)
    kh = k.reshape(B, S, H, N).astype(jnp.float32)
    vh = v.reshape(B, S, H, N).astype(jnp.float32)
    ah = a.reshape(B, S, H, N).astype(jnp.float32)
    y = wkv7_scan(rh, decay.reshape(B, S, H, N), kh, vh, -kk, kk * ah)
    mu = jnp.mean(y, axis=-1, keepdims=True)
    var = jnp.mean(jnp.square(y - mu), axis=-1, keepdims=True)
    yn = ((y - mu) * lax.rsqrt(var + RWKV_GN_EPS)).reshape(B, S, RW)
    yn = yn * ln_w.astype(jnp.float32) + ln_b.astype(jnp.float32)
    bonus = (jnp.sum(rh * kh * r_k.astype(jnp.float32), axis=-1, keepdims=True) * vh).reshape(B, S, RW)
    return ((yn + bonus) * g.astype(jnp.float32)).astype(z.dtype) @ w_out

def hybrid_mixer(h, positions, w_in, gate_bias, attn_w_up, rwkv_mu, rwkv_w0, rwkv_w2, rwkv_a0,
                 rwkv_a2, rwkv_g2, rwkv_k_k, rwkv_k_a, rwkv_r_k, rwkv_ln_w, rwkv_ln_b,
                 rwkv_w_out, w_o):
    proj = h @ w_in
    aw, rs = 3 * ATTN_WIDTH, RWKV_STREAM
    gates = jax.nn.sigmoid(proj[..., aw + rs:] + gate_bias)
    y_attn = dilated_attention(proj[..., :aw], positions) @ attn_w_up
    y_rwkv = rwkv7_time_mix(token_shift(proj[..., aw:aw + rs], rwkv_mu), rwkv_w0, rwkv_w2,
                            rwkv_a0, rwkv_a2, rwkv_g2, rwkv_k_k, rwkv_k_a, rwkv_r_k,
                            rwkv_ln_w, rwkv_ln_b, rwkv_w_out)
    merged = gates[..., :D_MODEL] * y_attn + gates[..., D_MODEL:] * y_rwkv
    return merged @ w_o

def first_inputs(seed: int = 0) -> dict:
    key = jax.random.key(seed)
    ks = iter(jax.random.split(key, 40))
    f32 = jnp.float32

    def nrm(shape, scale):
        return jax.random.normal(next(ks), shape, f32) * scale

    def gain(shape):
        return 1.0 + 0.05 * jax.random.normal(next(ks), shape, f32)

    L, D, F = DEPTH, D_MODEL, D_FF
    RW, H, N = RWKV_WIDTH, RWKV_HEADS, RWKV_HEAD_DIM
    return {
        'x': nrm((BATCH, SEQ, D), 1.0),
        'ffn1_norm': gain((L, D)),
        'ffn1_w_gate': nrm((L, D, F), D ** -0.5),
        'ffn1_w_up': nrm((L, D, F), D ** -0.5),
        'ffn1_w_down': nrm((L, F, D), F ** -0.5),
        'mix_norm': gain((L, D)),
        'w_in': nrm((L, D, IN_COLS), D ** -0.5),
        'gate_bias': nrm((L, 2 * D), 0.1),
        'attn_w_up': nrm((L, ATTN_OUT_WIDTH, D), ATTN_OUT_WIDTH ** -0.5),
        'rwkv_mu': jax.random.uniform(next(ks), (L, RWKV_STREAM), f32),
        'rwkv_w0': jax.random.uniform(next(ks), (L, RW), f32, -6.0, -1.0),
        'rwkv_w2': nrm((L, DECAY_LORA, RW), 0.1 * DECAY_LORA ** -0.5),
        'rwkv_a0': nrm((L, RW), 0.1),
        'rwkv_a2': nrm((L, ICLR_LORA, RW), 0.1 * ICLR_LORA ** -0.5),
        'rwkv_g2': nrm((L, GATE_LORA, RW), GATE_LORA ** -0.5),
        'rwkv_k_k': 0.85 + 0.05 * jax.random.normal(next(ks), (L, RW), f32),
        'rwkv_k_a': gain((L, RW)),
        'rwkv_r_k': nrm((L, H, N), 0.1),
        'rwkv_ln_w': gain((L, RW)),
        'rwkv_ln_b': nrm((L, RW), 0.02),
        'rwkv_w_out': nrm((L, RW, D), RW ** -0.5),
        'w_o': nrm((L, D, D), D ** -0.5),
        'ffn2_norm': gain((L, D)),
        'ffn2_w_gate': nrm((L, D, F), D ** -0.5),
        'ffn2_w_up': nrm((L, D, F), D ** -0.5),
        'ffn2_w_down': nrm((L, F, D), F ** -0.5),
        'final_norm': gain((D,)),
    }

def first_block(x, ffn1_norm, ffn1_w_gate, ffn1_w_up, ffn1_w_down, mix_norm, w_in, gate_bias,
              attn_w_up, rwkv_mu, rwkv_w0, rwkv_w2, rwkv_a0, rwkv_a2, rwkv_g2, rwkv_k_k,
              rwkv_k_a, rwkv_r_k, rwkv_ln_w, rwkv_ln_b, rwkv_w_out, w_o, ffn2_norm,
              ffn2_w_gate, ffn2_w_up, ffn2_w_down, final_norm):
    positions = jnp.arange(x.shape[1], dtype=jnp.int32)
    for layer in range(DEPTH):
        x = x + 0.5 * swiglu(rms_norm(x, ffn1_norm[layer]), ffn1_w_gate[layer],
                             ffn1_w_up[layer], ffn1_w_down[layer])
        x = x + hybrid_mixer(rms_norm(x, mix_norm[layer]), positions, w_in[layer],
                             gate_bias[layer], attn_w_up[layer], rwkv_mu[layer],
                             rwkv_w0[layer], rwkv_w2[layer], rwkv_a0[layer], rwkv_a2[layer],
                             rwkv_g2[layer], rwkv_k_k[layer], rwkv_k_a[layer],
                             rwkv_r_k[layer], rwkv_ln_w[layer], rwkv_ln_b[layer],
                             rwkv_w_out[layer], w_o[layer])
        x = x + 0.5 * swiglu(rms_norm(x, ffn2_norm[layer]), ffn2_w_gate[layer],
                             ffn2_w_up[layer], ffn2_w_down[layer])
    return rms_norm(x, final_norm)


DEPTH_2 = 2

N_A_LAYERS = DEPTH_2 // 2
N_B_LAYERS = DEPTH_2 - N_A_LAYERS
RET_HEADS = 4
RET_QK_DIM = D_MODEL // RET_HEADS
RET_V_DIM = 2 * RET_QK_DIM
RET_CHUNK = 128
RET_ROT_BASE = 10000.0
ATT_HEADS = 8
ATT_HEAD_DIM = D_MODEL // ATT_HEADS
ROPE_DIM_2 = ATT_HEAD_DIM // 4
MOBA_BLOCK = 256
MOBA_TOPK = 3
MOBA_Q_CHUNK = 32
N_GROUPS = 4
EXPERTS_PER_GROUP = 4
D_EXPERT = D_MODEL // 2
EXPERT_TOPK = 2


def rms_norm_2(x, g):
    x32 = x.astype(jnp.float32)
    y = x32 * lax.rsqrt(jnp.mean(x32 * x32, axis=-1, keepdims=True) + NORM_EPS)
    return (y * g.astype(jnp.float32)).astype(x.dtype)

def rotary(x, pos, rot_dim, theta):
    half = rot_dim // 2
    inv = 1.0 / (theta ** (jnp.arange(half, dtype=jnp.float32) / half))
    ang = pos.astype(jnp.float32)[:, None] * inv[None, :]
    cos = jnp.cos(ang)[:, None, :]
    sin = jnp.sin(ang)[:, None, :]
    xr = x[..., :rot_dim].astype(jnp.float32)
    x1, x2 = xr[..., :half], xr[..., half:]
    rot = jnp.concatenate([x1 * cos - x2 * sin, x2 * cos + x1 * sin], axis=-1).astype(x.dtype)
    return jnp.concatenate([rot, x[..., rot_dim:]], axis=-1)

def retention(x, w_in, w_out):
    B, S, _ = x.shape
    H, dk, dv, C = RET_HEADS, RET_QK_DIM, RET_V_DIM, RET_CHUNK
    f32 = jnp.float32
    proj = x @ w_in
    q, k, v, g = jnp.split(proj, [H * dk, 2 * H * dk, 2 * H * dk + H * dv], axis=-1)
    pos = jnp.arange(S)
    q = rotary(q.reshape(B, S, H, dk), pos, dk, RET_ROT_BASE)
    k = rotary(k.reshape(B, S, H, dk), pos, dk, RET_ROT_BASE) * (dk ** -0.5)
    v = v.reshape(B, S, H, dv)
    n_c = S // C
    qc = q.astype(f32).reshape(B, n_c, C, H, dk).transpose(1, 0, 3, 2, 4)
    kc = k.astype(f32).reshape(B, n_c, C, H, dk).transpose(1, 0, 3, 2, 4)
    vc = v.astype(f32).reshape(B, n_c, C, H, dv).transpose(1, 0, 3, 2, 4)
    log_gamma = jnp.log1p(-jnp.power(2.0, -5.0 - jnp.arange(H, dtype=f32)))
    idx = jnp.arange(C, dtype=f32)
    diff = idx[:, None] - idx[None, :]
    decay_mask = jnp.where(diff >= 0, jnp.exp(log_gamma[:, None, None] * jnp.maximum(diff, 0.0)), 0.0)
    q_decay = jnp.exp(log_gamma[:, None] * (idx + 1.0))
    k_decay = jnp.exp(log_gamma[:, None] * (C - 1.0 - idx))
    chunk_decay = jnp.exp(log_gamma * C)
    scores = jnp.einsum('nbhcd,nbhmd->nbhcm', qc, kc) * decay_mask[None, None]
    o_intra = jnp.einsum('nbhcm,nbhme->nbhce', scores, vc)

    def step(state, inp):
        qi, ki, vi = inp
        o = jnp.einsum('bhcd,bhde->bhce', qi * q_decay[None, :, :, None], state)
        state = state * chunk_decay[None, :, None, None] + jnp.einsum(
            'bhcd,bhce->bhde', ki * k_decay[None, :, :, None], vi)
        return state, o

    state0 = jnp.zeros((B, H, dk, dv), f32)
    _, o_cross = lax.scan(step, state0, (qc, kc, vc))
    o = (o_intra + o_cross).transpose(1, 0, 3, 2, 4).reshape(B, S, H, dv)
    o = o * lax.rsqrt(jnp.mean(o * o, axis=-1, keepdims=True) + NORM_EPS)
    y = jax.nn.silu(g.astype(f32)) * o.reshape(B, S, H * dv)
    return y.astype(x.dtype) @ w_out

def shared_kv(h, kv_norm, w_kv):
    B, S, _ = h.shape
    H, dh, BLK = ATT_HEADS, ATT_HEAD_DIM, MOBA_BLOCK
    hn = rms_norm_2(h, kv_norm)
    k, v = jnp.split(hn @ w_kv, 2, axis=-1)
    k = rotary(k.reshape(B, S, H, dh), jnp.arange(S), ROPE_DIM_2, ROPE_THETA)
    v = v.reshape(B, S, H, dh)
    n_blk = -(-S // BLK)
    pad = n_blk * BLK - S
    k = jnp.pad(k, ((0, 0), (0, pad), (0, 0), (0, 0))).transpose(0, 2, 1, 3).reshape(B, H, n_blk, BLK, dh)
    v = jnp.pad(v, ((0, 0), (0, pad), (0, 0), (0, 0))).transpose(0, 2, 1, 3).reshape(B, H, n_blk, BLK, dh)
    k_mean = jnp.mean(k.astype(jnp.float32), axis=3).astype(k.dtype)
    return k, v, k_mean

def moba_attention(x, w_q, w_o, kb, vb, k_mean):
    B, S, _ = x.shape
    H, dh, BLK, QC = ATT_HEADS, ATT_HEAD_DIM, MOBA_BLOCK, MOBA_Q_CHUNK
    n_blk = kb.shape[2]
    s_pad = n_blk * BLK
    topk = min(MOBA_TOPK, n_blk)
    q = (x @ w_q).reshape(B, S, H, dh)
    q = rotary(q, jnp.arange(S), ROPE_DIM_2, ROPE_THETA) * (dh ** -0.5)
    q = jnp.pad(q, ((0, 0), (0, s_pad - S), (0, 0), (0, 0))).transpose(0, 2, 1, 3)
    n_qc = s_pad // QC
    qs = q.reshape(B, H, n_qc, QC, dh).transpose(2, 0, 1, 3, 4)
    b_idx = jnp.arange(B)[:, None, None, None]
    h_idx = jnp.arange(H)[None, :, None, None]
    blk_ids = jnp.arange(n_blk)
    neg_inf = -jnp.inf

    def attend(args):
        qi, ci = args
        q0 = ci * QC
        blk = q0 // BLK
        gate = jnp.einsum('bhqd,bhnd->bhqn', qi, k_mean).astype(jnp.float32)
        gate = jnp.where(blk_ids < blk, gate, neg_inf)
        _, sel = lax.top_k(gate, topk)
        slot_ok = jnp.arange(topk) < blk
        ks = kb[b_idx, h_idx, sel]
        vs = vb[b_idx, h_idx, sel]
        s_sel = jnp.einsum('bhqd,bhqnkd->bhqnk', qi, ks).astype(jnp.float32)
        s_sel = jnp.where(slot_ok[:, None], s_sel, neg_inf).reshape(B, H, QC, topk * BLK)
        k_own = lax.dynamic_index_in_dim(kb, blk, axis=2, keepdims=False)
        v_own = lax.dynamic_index_in_dim(vb, blk, axis=2, keepdims=False)
        s_own = jnp.einsum('bhqd,bhkd->bhqk', qi, k_own).astype(jnp.float32)
        q_pos = q0 + jnp.arange(QC)
        k_pos = blk * BLK + jnp.arange(BLK)
        s_own = jnp.where(k_pos[None, :] <= q_pos[:, None], s_own, neg_inf)
        p = jax.nn.softmax(jnp.concatenate([s_sel, s_own], axis=-1), axis=-1).astype(vb.dtype)
        p_sel = p[..., :topk * BLK].reshape(B, H, QC, topk, BLK)
        p_own = p[..., topk * BLK:]
        return (jnp.einsum('bhqnk,bhqnkd->bhqd', p_sel, vs)
                + jnp.einsum('bhqk,bhkd->bhqd', p_own, v_own))

    o = lax.map(attend, (qs, jnp.arange(n_qc)))
    o = o.transpose(1, 0, 3, 2, 4).reshape(B, s_pad, H * dh)[:, :S]
    return o @ w_o

def hier_moe(x, w_rg, b_rg, w_re, b_re, w_gate, w_up, w_down):
    B, S, D = x.shape
    G, E = N_GROUPS, EXPERTS_PER_GROUP
    t = x.reshape(-1, D)
    g_prob = jax.nn.softmax((t @ w_rg).astype(jnp.float32) + b_rg, axis=-1)
    g_val, g_idx = lax.top_k(g_prob, 1)
    e_logits_all = jnp.einsum('td,gde->tge', t, w_re).astype(jnp.float32) + b_re
    e_logits = jnp.take_along_axis(e_logits_all, g_idx[:, :, None], axis=1)[:, 0]
    e_val, e_idx = lax.top_k(e_logits, EXPERT_TOPK)
    e_w = jax.nn.softmax(e_val, axis=-1)
    within = jnp.sum(jax.nn.one_hot(e_idx, E) * e_w[..., None], axis=1)
    group_w = jax.nn.one_hot(g_idx[:, 0], G) * g_val
    combine = (group_w[:, :, None] * within[:, None, :]).astype(x.dtype)
    y = jnp.zeros_like(t)
    for g in range(G):
        hg = jax.nn.silu(jnp.einsum('td,edf->tef', t, w_gate[g])) * jnp.einsum('td,edf->tef', t, w_up[g])
        y = y + jnp.einsum('tef,efd->td', hg * combine[:, g, :, None], w_down[g])
    return y.reshape(B, S, D)

def second_inputs(seed: int = 0) -> dict:
    key = jax.random.key(seed)
    ks = jax.random.split(key, 18)
    f32 = jnp.float32

    def normal(k, shape, scale):
        return jax.random.normal(k, shape, f32) * scale

    def gain(k, shape):
        return 1.0 + 0.05 * jax.random.normal(k, shape, f32)

    out_scale = (2.0 * DEPTH_2) ** -0.5
    ret_in_cols = 2 * RET_HEADS * RET_QK_DIM + 2 * RET_HEADS * RET_V_DIM
    att_w = ATT_HEADS * ATT_HEAD_DIM
    return {
        'x': normal(ks[0], (BATCH, SEQ, D_MODEL), 1.0),
        'ret_norm': gain(ks[1], (N_A_LAYERS, D_MODEL)),
        'ret_w_in': normal(ks[2], (N_A_LAYERS, D_MODEL, ret_in_cols), D_MODEL ** -0.5),
        'ret_w_out': normal(ks[3], (N_A_LAYERS, RET_HEADS * RET_V_DIM, D_MODEL), (RET_HEADS * RET_V_DIM) ** -0.5 * out_scale),
        'kv_norm': gain(ks[4], (D_MODEL,)),
        'w_kv': normal(ks[5], (D_MODEL, 2 * att_w), D_MODEL ** -0.5),
        'attn_norm': gain(ks[6], (N_B_LAYERS, D_MODEL)),
        'w_q': normal(ks[7], (N_B_LAYERS, D_MODEL, att_w), D_MODEL ** -0.5),
        'w_o': normal(ks[8], (N_B_LAYERS, att_w, D_MODEL), att_w ** -0.5 * out_scale),
        'ffn_norm': gain(ks[9], (DEPTH_2, D_MODEL)),
        'router_group_w': normal(ks[10], (DEPTH_2, D_MODEL, N_GROUPS), D_MODEL ** -0.5),
        'router_group_b': normal(ks[11], (DEPTH_2, N_GROUPS), 0.01),
        'router_expert_w': normal(ks[12], (DEPTH_2, N_GROUPS, D_MODEL, EXPERTS_PER_GROUP), D_MODEL ** -0.5),
        'router_expert_b': normal(ks[13], (DEPTH_2, N_GROUPS, EXPERTS_PER_GROUP), 0.01),
        'expert_w_gate': normal(ks[14], (DEPTH_2, N_GROUPS, EXPERTS_PER_GROUP, D_MODEL, D_EXPERT), D_MODEL ** -0.5),
        'expert_w_up': normal(ks[15], (DEPTH_2, N_GROUPS, EXPERTS_PER_GROUP, D_MODEL, D_EXPERT), D_MODEL ** -0.5),
        'expert_w_down': normal(ks[16], (DEPTH_2, N_GROUPS, EXPERTS_PER_GROUP, D_EXPERT, D_MODEL), D_EXPERT ** -0.5 * out_scale),
        'final_norm': gain(ks[17], (D_MODEL,)),
    }

def second_block(x, ret_norm, ret_w_in, ret_w_out, kv_norm, w_kv, attn_norm, w_q, w_o,
              ffn_norm, router_group_w, router_group_b, router_expert_w, router_expert_b,
              expert_w_gate, expert_w_up, expert_w_down, final_norm):
    h = x
    kb = vb = k_mean = None
    for layer in range(DEPTH_2):
        if layer < N_A_LAYERS:
            h = h + retention(rms_norm_2(h, ret_norm[layer]), ret_w_in[layer], ret_w_out[layer])
        else:
            if layer == N_A_LAYERS:
                kb, vb, k_mean = shared_kv(h, kv_norm, w_kv)
            j = layer - N_A_LAYERS
            h = h + moba_attention(rms_norm_2(h, attn_norm[j]), w_q[j], w_o[j], kb, vb, k_mean)
        h = h + hier_moe(rms_norm_2(h, ffn_norm[layer]), router_group_w[layer], router_group_b[layer],
                         router_expert_w[layer], router_expert_b[layer], expert_w_gate[layer],
                         expert_w_up[layer], expert_w_down[layer])
    return rms_norm_2(h, final_norm)


def setup_inputs(seed=0):
    out = dict(first_inputs(seed))
    for name, value in second_inputs(seed + 1).items():
        if name != "x":
            out[name + "_2"] = value
    return out


def reference(
    x, ffn1_norm, ffn1_w_gate, ffn1_w_up, ffn1_w_down, mix_norm, w_in, gate_bias, attn_w_up,
    rwkv_mu, rwkv_w0, rwkv_w2, rwkv_a0, rwkv_a2, rwkv_g2, rwkv_k_k, rwkv_k_a, rwkv_r_k,
    rwkv_ln_w, rwkv_ln_b, rwkv_w_out, w_o, ffn2_norm, ffn2_w_gate, ffn2_w_up, ffn2_w_down,
    final_norm, ret_norm_2, ret_w_in_2, ret_w_out_2, kv_norm_2, w_kv_2, attn_norm_2, w_q_2,
    w_o_2, ffn_norm_2, router_group_w_2, router_group_b_2, router_expert_w_2, router_expert_b_2,
    expert_w_gate_2, expert_w_up_2, expert_w_down_2, final_norm_2,
):
    x = first_block(
        x, ffn1_norm, ffn1_w_gate, ffn1_w_up, ffn1_w_down, mix_norm, w_in, gate_bias, attn_w_up,
        rwkv_mu, rwkv_w0, rwkv_w2, rwkv_a0, rwkv_a2, rwkv_g2, rwkv_k_k, rwkv_k_a, rwkv_r_k,
        rwkv_ln_w, rwkv_ln_b, rwkv_w_out, w_o, ffn2_norm, ffn2_w_gate, ffn2_w_up, ffn2_w_down,
        final_norm,
    )
    return second_block(
        x, ret_norm_2, ret_w_in_2, ret_w_out_2, kv_norm_2, w_kv_2, attn_norm_2, w_q_2, w_o_2,
        ffn_norm_2, router_group_w_2, router_group_b_2, router_expert_w_2, router_expert_b_2,
        expert_w_gate_2, expert_w_up_2, expert_w_down_2, final_norm_2,
    )


_drawn_inputs = setup_inputs


def setup_inputs(seed=0):
    import zlib

    import numpy as np

    out = dict(_drawn_inputs(seed))
    spreads = {}
    factors = {'gate_bias': 2.723,
     'rwkv_w2': 8.0,
     'kv_norm_2': 8.0,
     'attn_norm_2': 8.0,
     'router_group_b_2': 6.315,
     'router_expert_b_2': 6.409}
    for name, (base, spread) in spreads.items():
        noise = np.random.default_rng([zlib.crc32(name.encode()), seed]).standard_normal(out[name].shape)
        drawn = base * np.exp(spread * noise) if base else spread * noise
        out[name] = jnp.asarray(drawn.astype(out[name].dtype))
    for name, factor in factors.items():
        out[name] = (out[name] * factor).astype(out[name].dtype)
    return out
```

```python
from contextlib import ExitStack
import math

import numpy as np
import concourse.bass as bass
from concourse import mybir

F32 = mybir.dt.float32
ALU = mybir.AluOpType
ACT = mybir.ActivationFunctionType
AX = mybir.AxisListType

P = 128
T = 256
NT = T // P
D = 1024
KT = D // P
CH = 2048
CC = CH // KT
RING = 6
EPS = 1e-6

FFN_GROUPS = 2816 // CC
EXPERTS, D_EXPERT = 16, 512
MOE_GROUPS = EXPERTS * D_EXPERT // CC

DIL_HEADS, DIL_GROUPS, DIL_DH = 4, 3, 64
RW_HEADS, RW_N = 16, 64
PAIRS = RW_HEADS // 2
RET_HEADS, RET_DK, RET_DV = 4, 256, 512
MOBA_HEADS, MOBA_DH = 8, 128
AW = 3 * DIL_GROUPS * DIL_HEADS * DIL_DH
AQ = AW // 3
RS = 3 * D + 64 + 64 + 160
DECAY = math.exp(-0.5)
MASKED = -1e30



def swiglu_order(groups):
    order = [("gate", 0), ("up", 0)]
    for j in range(1, groups):
        order += [("gate", j), ("up", j), ("down", j - 1)]
    return order + [("down", groups - 1)]


PHASES = [
    ("ffn1", 3 * FFN_GROUPS),
    ("dil_qk", 2 * AQ // CC),
    ("dil_v", 4),
    ("lora", 1), ("lora_rest", 1), ("lora_g", 1),
    ("rkv", 3 * D // CC),
    ("gate_a", 4), ("gate_r", 4),
    ("attn_up", 1),
    ("rwkv_out", 4),
    ("mix_out", 4),
    ("ffn2", 3 * FFN_GROUPS),
    ("ret_qk", 2 * D // CC),
    ("ret_v", 8), ("ret_g", 8),
    ("ret_out", 8),
    ("moe0", 3 * MOE_GROUPS),
    ("moba_k", 4), ("moba_v", 4), ("moba_q", 4), ("moba_out", 4),
    ("moe1", 3 * MOE_GROUPS),
]
START = {}
NCHUNK = 0
for _name, _n in PHASES:
    START[_name] = NCHUNK
    NCHUNK += _n
assert NCHUNK % RING == 0

ACC = {n: i for i, n in enumerate(
    ["ffn1", "dil_v", "gate_a", "gate_r", "attn_up", "rwkv_out", "mix_out", "ffn2", "ret_v0", "ret_v1",
     "ret_g0", "ret_g1", "ret_out", "moe0", "moba_v", "moba_out", "moe1"])}
NORM = {n: i for i, n in enumerate(["ffn1", "mix", "ffn2", "mid", "ret", "moe0", "moba", "moe1", "final"])}
TURN = {n: i for i, n in enumerate(["ffn1", "mix", "ffn2", "ret", "moe0", "moba", "moe1"])}
GROUP0 = {"ffn1": 0, "ffn2": FFN_GROUPS, "moe0": 2 * FFN_GROUPS, "moe1": 2 * FFN_GROUPS + MOE_GROUPS}
ROPE0 = {"dil": 0, "moba_k": 6, "moba_q": 10}
ATT0 = {"dil": 0, "moba": 8}


def columns_chunk(w, c0, n=CC):
    return w[:, c0:c0 + n].reshape(KT, P, n).transpose(1, 0, 2).reshape(P, KT * n)


def rows_chunk(w, r0):
    part = w[r0:r0 + 2 * P].reshape(2, P, w.shape[1]).transpose(1, 0, 2)
    return np.pad(part, ((0, 0), (0, 0), (0, D - w.shape[1]))).reshape(P, CH)


def weight_stream(w):
    out = []

    def put(a):
        out.append(np.pad(a, ((0, P - a.shape[0]), (0, CH - a.shape[1]))))

    def gated(gate, up, down, groups):
        for kind, j in swiglu_order(groups):
            if kind == "down":
                put(rows_chunk(down, j * CC))
            else:
                put(columns_chunk(gate if kind == "gate" else up, j * CC))

    def rows(m):
        for r in range(0, m.shape[0], 2 * P):
            put(rows_chunk(m, r))

    def cols(m):
        for c in range(0, m.shape[1], CC):
            put(columns_chunk(m, c))

    gated(w["ffn1_w_gate"][0], w["ffn1_w_up"][0], w["ffn1_w_down"][0], FFN_GROUPS)
    w_in = w["w_in"][0]
    cols(w_in[:, :2 * AQ])
    rows(w_in[:, 2 * AQ:AW])
    lora = w_in[:, AW + 3 * D:AW + RS]
    put(columns_chunk(lora, 0))
    put(np.concatenate([columns_chunk(lora, CC, 32),
                        np.concatenate([w["rwkv_w2"][0], w["rwkv_a2"][0]], 0)], 1))
    g2 = w["rwkv_g2"][0]
    put(np.concatenate([g2[:P], np.pad(g2[P:], ((0, P - 32), (0, 0)))], 1))
    cols(w_in[:, AW:AW + 3 * D])
    rows(w_in[:, AW + RS:AW + RS + D])
    rows(w_in[:, AW + RS + D:])
    rows(w["attn_w_up"][0])
    rows(w["rwkv_w_out"][0])
    rows(w["w_o"][0])
    gated(w["ffn2_w_gate"][0], w["ffn2_w_up"][0], w["ffn2_w_down"][0], FFN_GROUPS)
    ret = w["ret_w_in_2"][0]
    cols(ret[:, :2 * D])
    for c in range(2 * D, 6 * D, D):
        rows(ret[:, c:c + D])
    rows(w["ret_w_out_2"][0])

    def moe(layer):
        g, u, d = (w[f"expert_w_{n}_2"][layer].reshape(EXPERTS, *w[f"expert_w_{n}_2"].shape[3:])
                   for n in ("gate", "up", "down"))
        per = D_EXPERT // CC
        for kind, j in swiglu_order(MOE_GROUPS):
            e, c = j // per, j % per * CC
            put(rows_chunk(d[e], c) if kind == "down" else columns_chunk((g if kind == "gate" else u)[e], c))

    moe(0)
    cols(w["w_kv_2"][:, :D])
    rows(w["w_kv_2"][:, D:])
    cols(w["w_q_2"][0])
    rows(w["w_o_2"][0])
    moe(1)
    assert len(out) == NCHUNK
    return np.stack(out)



VECTORS = ["ffn1_norm", "mix_norm", "ffn2_norm", "ret_norm_2", "kv_norm_2", "attn_norm_2", "rwkv_w0",
           "rwkv_a0", "rwkv_k_k", "rwkv_k_a", "rwkv_r_k", "rwkv_ln_w", "rwkv_ln_b"]
PARAM = {}
_at = 0
for _name in VECTORS + ["ffn_norm_0", "ffn_norm_1"]:
    PARAM[_name] = _at
    _at += KT
PARAM["mu"] = _at
_at += 27
ROUTE = 20
for _l in range(2):
    PARAM[f"route_w{_l}"] = _at
    _at += KT * ROUTE
    PARAM[f"route_b{_l}"] = _at
    _at += ROUTE
NPARAM = _at


def param_table(w):
    def column(v):
        return np.asarray(v).reshape(KT, P).T

    parts = [column(w[n]) for n in VECTORS] + [column(w["ffn_norm_2"][l]) for l in range(2)]
    mu = w["rwkv_mu"][0]
    parts.append(mu[:3 * D].reshape(24, P).T)
    lora = np.pad(mu[3 * D:], (0, 3 * P - 288)).reshape(3, P).T
    parts.append(lora)
    for l in range(2):
        rw = np.concatenate([w["router_group_w_2"][l],
                             w["router_expert_w_2"][l].transpose(1, 0, 2).reshape(D, 16)], 1)
        parts.append(rw.reshape(KT, P, ROUTE).transpose(1, 0, 2).reshape(P, KT * ROUTE))
        rb = np.concatenate([w["router_group_b_2"][l], w["router_expert_b_2"][l].reshape(16)])
        parts.append(np.broadcast_to(rb, (P, ROUTE)))
    return np.concatenate(parts, 1)



CONST = {}
_at = 0
for _name, _n in [("ident", P), ("head_ones", P), ("dil_swap", P), ("moba_swap", P),
                  ("dil_cos", T), ("dil_sin", T), ("ret_cos", T), ("ret_sin", T), ("moba_cos", T),
                  ("moba_sin", T), ("dil_mask0", 3 * P), ("dil_mask1", 3 * T), ("causal0", P),
                  ("causal1", T), ("tri_up", T), ("blk_up", P), ("blk_low", P), ("off_low", P),
                  ("ret_decay", RET_HEADS * 3 * P)]:
    CONST[_name] = (_at, _n)
    _at += _n
NCONST = _at


def const_table():
    c = np.zeros((P, NCONST), np.float32)

    def put(name, a):
        at, n = CONST[name]
        c[:, at:at + n] = np.asarray(a, np.float64).reshape(P, n)

    i = np.arange(P)
    put("ident", np.eye(P))
    put("head_ones", (i[:, None] // 64 == i[None] // 64))
    pos = np.arange(T, dtype=np.float32)

    def rope(inv_freq, dh, half):
        ang = (pos[None, :] * inv_freq[:, None].astype(np.float32)).astype(np.float32)
        cos, sin, swap = np.ones((P, T)), np.zeros((P, T)), np.zeros((P, P))
        for a in range(P):
            d = a % dh
            if d < half:
                cos[a], sin[a], swap[a + half, a] = np.cos(ang[d]), -np.sin(ang[d]), 1
            elif d < 2 * half:
                cos[a], sin[a], swap[a - half, a] = np.cos(ang[d - half]), np.sin(ang[d - half]), 1
        return cos, sin, swap

    theta = np.float32(500000.0)
    cos, sin, swap = rope(np.power(theta, -np.arange(8, dtype=np.float32) * np.float32(2.0 / 16)), 64, 8)
    put("dil_cos", cos), put("dil_sin", sin), put("dil_swap", swap)
    cos, sin, swap = rope(np.float32(1) / theta ** (np.arange(16, dtype=np.float32) / np.float32(16)), 128, 16)
    put("moba_cos", cos), put("moba_sin", sin), put("moba_swap", swap)
    inv = np.float32(1) / np.float32(10000.0) ** (np.arange(128, dtype=np.float32) / np.float32(128))
    ang = (pos[None, :] * inv[:, None]).astype(np.float32)
    put("ret_cos", np.cos(ang)), put("ret_sin", np.sin(ang))
    for tile in range(NT):
        t = tile * P + i[:, None]
        s = np.arange(P * (tile + 1))[None]
        ok = [(t >= s) & ((t - s) % dil == 0) & (t - s <= win) for win, dil in ((128, 1), (512, 4), (2048, 16))]
        put(f"dil_mask{tile}", np.where(np.concatenate(ok, 1), 0.0, MASKED))
        put(f"causal{tile}", np.where(t >= s, 0.0, MASKED))
    up, same = i[:, None] < i[None], i[:, None] // 16 == i[None] // 16
    put("tri_up", np.concatenate([up, i[:, None] <= i[None]], 1))
    put("blk_up", up & same)
    put("blk_low", up.T & same)
    put("off_low", up.T & ~same)
    decay = []
    for h in range(RET_HEADS):
        gamma = np.log1p(-np.power(2.0, -5.0 - h))
        for off in (0, P, 0):
            diff = i[None] + off - i[:, None]
            decay.append(np.where(diff >= 0, np.exp(gamma * np.maximum(diff, 0)), 0.0) * RET_DK ** -0.5)
    put("ret_decay", np.concatenate(decay, 1))
    return c


class Steps:

    def __init__(self, eng, sem):
        self.eng, self.sem, self.n = eng, sem, 0

    def did(self, ins):
        ins.then_inc(self.sem, 1)
        self.n += 1

    def settle(self):
        self.eng.wait_ge(self.sem, self.n)




def two_blocks(nc, stream, params, consts, x_in, gate_bias, gains, out):
    ctx = ExitStack()
    with ctx:
        def sb(name, *shape):
            return ctx.enter_context(nc.sbuf_tensor(name, [P, *shape], F32))

        def sem(name):
            return ctx.enter_context(nc.semaphore(name))

        ring = sb("ring", RING, CH)
        par = sb("par", NPARAM)
        con = sb("con", NCONST)
        x = sb("x", NT, D)
        xnT = sb("xnT", KT, T)
        small = sb("small", 224)
        ones = sb("ones", P)
        attT = sb("attT", 2, T)
        NA = 14
        arena = sb("arena", NA, CH)
        ps = ctx.enter_context(nc.psum_tensor("ps", [P, 8, 512], F32))
        wk = [ps[:, b, :] for b in range(4)]
        acc = [ps[:, 4 + b, :] for b in range(4)]
        accf = ps[:, 4:8, :].rearrange("p b n -> p (b n)")
        wkf = ps[:, 0:4, :].rearrange("p b n -> p (b n)")

        def A(i, n=1):
            return arena[:, i:i + n, :].rearrange("p a n -> p (a n)")

        def con_(name):
            at, n = CONST[name]
            return con[:, at:at + n]

        def par_(name, n=KT):
            return par[:, PARAM[name]:PARAM[name] + n]

        ident = con_("ident")
        xn = A(NA - 1).rearrange("p (t d) -> p t d", t=NT)
        junk = A(NA - 2).rearrange("p (t d) -> p t d", t=NT)
        ss, std, rstd = small[:, 0:2], small[:, 2:4], small[:, 4:6]
        sil = A(NA - 2)[:, 0:1024].rearrange("p (a f t) -> p a f t", a=2, f=2)
        hidT = A(NA - 2)[:, 1024:2048].rearrange("p (a f t) -> p a f t", a=2, f=2)

        landed = [sem(f"chunk_landed{s}") for s in range(RING)]
        chunks_used = sem("chunks_used")
        x_loaded, tables_loaded, gain_loaded, bias_loaded = (sem(n) for n in (
            "x_loaded", "tables_loaded", "gain_loaded", "bias_loaded"))
        acc_done, acc_read = sem("acc_done"), sem("acc_read")
        norm_sum, norm_std, norm_scaled, norm_turned = (sem(n) for n in (
            "norm_sum", "norm_std", "norm_scaled", "norm_turned"))
        xnT_by_dve, xnT_by_act = sem("xnT_by_dve"), sem("xnT_by_act")
        silu_done, hidden_ready, gated = sem("silu_done"), sem("hidden_ready"), sem("gated")
        rope_raw, rope_swapped, rope_used, rope_done = (sem(n) for n in (
            "rope_raw", "rope_swapped", "rope_used", "rope_done"))
        scores_ready, scores_read, bias_ready, exp_done, probs_ready, probs_turned, probsT_ready, heads_ready, \
            heads_read = (sem(n) for n in (
                "scores_ready", "scores_read", "bias_ready", "exp_done", "probs_ready", "probs_turned",
                "probsT_ready", "heads_ready", "heads_read"))
        dve_steps, act_steps = sem("dve_steps"), sem("act_steps")
        zeroed = sem("zeroed")
        rest_ready, z_copied, z_shifted = sem("rest_ready"), sem("z_copied"), sem("z_shifted")
        lora_act, lora_done, lora_by_act, lora_by_dve = (sem(n) for n in (
            "lora_act", "lora_done", "lora_by_act", "lora_by_dve"))
        kk_scaled, kk_squared, kk_summed, kk_root, kk_done = (sem(n) for n in (
            "kk_scaled", "kk_squared", "kk_summed", "kk_root", "kk_done"))
        cum_done, decays_done, rk_done, rk_summed, bonus_done, tilde_done, turned_vbk, v_tok, bk_tok = (sem(n) for n in (
            "cum_done", "decays_done", "rk_done", "rk_summed", "bonus_done", "tilde_done", "turned_vbk", "v_tok",
            "bk_tok"))
        lane_pe = [sem(f"lane_pe{i}") for i in range(4)]
        lane_dve = [sem(f"lane_dve{i}") for i in range(4)]
        lane_act = [sem(f"lane_act{i}") for i in range(4)]
        y_centred, y_squared, y_var, y_std, y_normed, y_turned, y_affine, z_done = (sem(n) for n in (
            "y_centred", "y_squared", "y_var", "y_std", "y_normed", "y_turned", "y_affine", "z_done"))
        x_scaled, rot_read, rot_done, rs_ready, rs_masked, o_ready, o_summed, o_std, ret_y_done, ret_turned, \
            ret_copied = (sem(n) for n in (
                "x_scaled", "rot_read", "rot_done", "rs_ready", "rs_masked", "o_ready", "o_summed", "o_std",
                "ret_y_done", "ret_turned", "ret_copied"))
        routed, route_shifted, route_exp, route_diff, route_exp2, combine_ready, combine_turned, weightT_ready, \
            spread, spread_read = (sem(n) for n in (
                "routed", "route_shifted", "route_exp", "route_diff", "route_exp2", "combine_ready",
                "combine_turned", "weightT_ready", "spread", "spread_read"))
        gate_done, merge_done, merge_turned, merge_copied = (sem(n) for n in (
            "gate_done", "merge_done", "merge_turned", "merge_copied"))
        stored_ready, stored = sem("stored_ready"), sem("stored")

        block = ctx.enter_context(nc.Block())

        def slot(c):
            return ring[:, c % RING, :]

        def cols_view(c, n=CC):
            return slot(c)[:, 0:KT * n].rearrange("p (k n) -> p k n", k=KT)

        def rows_view(c):
            return slot(c).rearrange("p (j n) -> p j n", j=2)

        shifted = A(11)[:, 0:2 * T].rearrange("p (f t) -> p f t", f=2)

        def lane_counts(g, st):
            dve = min(g, 4) * 9 + max(g - 4, 0) * 8 + sum(n <= st for n in (1, 3, 4, 5, 6, 7, 8, 9))
            dve += (st >= 10 and g < 4)
            return dve, 7 * g + sum(n <= st for n in (2, 3, 4, 6, 7, 8, 10))

        class Att:
            def __init__(self, base, heads, groups, dh, scale, mask, q, k, v, outT):
                self.units = [(h, i) for h in range(heads) for i in range(NT)]
                self.base, self.groups, self.dh, self.scale = base, groups, dh, scale
                self.mask, self.q, self.k, self.v, self.outT = mask, q, k, v, outT

            def width(self, i):
                return self.groups * P * (i + 1)

        dil_qk = A(0, 2)[:, 0:12 * T].rearrange("p (k t) -> p k t", k=12)
        dil_v = A(2)[:, 0:2 * AQ].rearrange("p (t n) -> p t n", t=NT)
        moba_k = A(0).rearrange("p (k t) -> p k t", k=KT)
        moba_v = A(1).rearrange("p (t n) -> p t n", t=NT)
        moba_q = A(2).rearrange("p (k t) -> p k t", k=KT)
        moba_oT = A(3).rearrange("p (k t) -> p k t", k=KT)
        xqT = A(4).rearrange("p (k t) -> p k t", k=KT)
        prob = A(5, 2).rearrange("p (a n) -> p a n", a=2)
        probT = A(7)[:, 0:768]
        raw = A(8)[:, 0:1024].rearrange("p (a n) -> p a n", a=2)
        turned = A(8)[:, 1024:2048].rearrange("p (a n) -> p a n", a=2)
        dil = Att(0, DIL_HEADS, 3, DIL_DH, DIL_DH ** -0.5, ("dil_mask0", "dil_mask1"),
                  lambda h, g: (dil_qk[64 * (h % 2):64 * (h % 2) + 64, 2 * g + h // 2, :]),
                  lambda h, g: (dil_qk[64 * (h % 2):64 * (h % 2) + 64, 6 + 2 * g + h // 2, :]),
                  lambda h, g, s: dil_v[:, s, (4 * g + h) * 64:(4 * g + h) * 64 + 64],
                  lambda h, i: attT[64 * (h % 2):64 * (h % 2) + 64, h // 2, i * P:i * P + P])
        moba = Att(8, MOBA_HEADS, 1, MOBA_DH, MOBA_DH ** -0.5, ("causal0", "causal1"),
                   lambda h, g: moba_q[:, h, :], lambda h, g: moba_k[:, h, :],
                   lambda h, g, s: moba_v[:, s, h * P:h * P + P],
                   lambda h, i: moba_oT[:, h, i * P:i * P + P])

        def pairs(i):
            return A(i).rearrange("p (k t) -> p k t", k=PAIRS)

        def by_chunk(i):
            return A(i).rearrange("p (a t) -> p a t", t=P)

        R8, K8, V8, KK8, A8, C8, E1, E2, B8, KD8, G8, BON = (pairs(i) for i in (0, 1, 2, 3, 4, 5, 6, 7, 10, 11, 12, 13))
        AR = A(8, 2).rearrange("p (a s t) -> p a s t", s=2, t=P)
        zraw = A(9)[:, 0:4 * (T + 1)].rearrange("p (a f t) -> p a f t", a=2, f=2)
        zlora = A(10)[:, 0:3 * T].rearrange("p (f t) -> p f t", f=3)
        Vtok = A(5).rearrange("p (c n) -> p c n", c=2)
        BKtok = A(6).rearrange("p (c n) -> p c n", c=2)
        Ytok = A(7).rearrange("p (c n) -> p c n", c=2)
        state = A(2)[:, 0:PAIRS * RW_N].rearrange("p (k n) -> p k n", k=PAIRS)
        lane = [A(i) for i in (0, 1, 3, 4)]
        mbk = [l[:, 0:512] for l in lane]
        XD = [l[:, 512:896].rearrange("p (a n) -> p a n", a=3) for l in lane]
        LO = [l[:, 896:1024] for l in lane]
        NN = [l[:, 1024:1280] for l in lane]
        NN2 = [l[:, 1280:1536] for l in lane]
        N4T = [l[:, 1536:1664] for l in lane]
        Wl = [l[:, 1664:1728] for l in lane]
        Ul = [l[:, 1728:1792] for l in lane]
        mid, endf, startf = small[:, 24:40], small[:, 40:48], small[:, 48:64]
        gsum, gvar = small[:, 64:96], small[:, 96:128]
        zT = pairs(1)
        gate_a, gate_r, gbias, merged, mergedT = (A(i) for i in (8, 9, 10, 11, 3))
        mpart = A(0)
        mergedT = mergedT.rearrange("p (k t) -> p k t", k=KT)
        head_ones = con_("head_ones")

        ret_q, ret_k = pairs(0), pairs(1)
        ret_v, ret_g, ret_y = (A(i, 2).rearrange("p (t n) -> p t n", t=NT) for i in (2, 4, 6))
        ret_yT = A(8, 2).rearrange("p (k t) -> p k t", t=T)
        ret_sT = A(10)[:, 0:4 * 384].rearrange("p (h n) -> p h n", h=RET_HEADS)
        ret_tmp = A(11).rearrange("p (a f t) -> p a f t", a=4, f=2)
        ret_ss, ret_std = small[:, 130:138], small[:, 138:146]
        by_expert = A(8, 2).rearrange("p (e t) -> p e t", e=EXPERTS)
        scratch = A(10)
        weightT = A(10)[:, 1024:1024 + T]
        gain_row = A(0)[:, 0:D]
        final_out = A(1).rearrange("p (t d) -> p t d", t=NT)

        @block.sync
        def _(sp):
            for s in range(RING):
                sp.dma_start(slot(s), stream[s]).then_inc(landed[s], 16)
            with sp.Fori(1, NCHUNK // RING) as i:
                for s in range(RING):
                    sp.wait_ge(chunks_used, i * RING + (s + 1 - RING))
                    sp.dma_start(slot(s), stream[bass.ds(i * RING + s, 1), :, :].rearrange("a p n -> p (a n)"))\
                        .then_inc(landed[s], 16)

        @block.tensor
        def _(pe):
            def wait_chunk(c, turn=None):
                n = 16 * (c // RING + 1)
                pe.wait_ge(landed[c % RING], n if turn is None else turn * 16 + n)

            def project(c, xT, bank, n=CC):
                w = cols_view(c, n)
                m = min(n, P)
                for f in range(max(n // P, 1)):
                    for k in range(KT):
                        mm = pe.matmul(bank[0:m, f * T:f * T + T], w[:, k, f * m:f * m + m], xT[:, k, :],
                                       start=(k == 0), stop=(k == KT - 1))
                mm.then_inc(chunks_used, 1)

            def accumulate(name, c, n, lhsT, width=D):
                use = ACC[name]
                for j in range(n):
                    wait_chunk(c + j)
                    w = rows_view(c + j)
                    for k in range(2):
                        for b in range(4):
                            tok, n0 = b // 2, b % 2 * 512
                            n1 = min(n0 + 512, width)
                            if j == 0 and k == 0 and use:
                                pe.wait_ge(acc_read, 4 * (use - 1) + b + 1)
                            mm = pe.matmul(acc[b][:, 0:n1 - n0], lhsT(2 * j + k)[:, tok * P:tok * P + P],
                                           w[:, k, n0:n1], start=(j == 0 and k == 0),
                                           stop=(j == n - 1 and k == 1))
                            if j == n - 1 and k == 1 and b < 3:
                                mm.then_inc(acc_done, 1)
                    mm.then_inc(chunks_used, 1)

            def norm(name, last_evac=True):
                n = NORM[name]
                for tok in range(NT):
                    pe.wait_ge(norm_scaled, NT * n + tok + 1)
                    for k in range(KT):
                        at = k % 2 * T + tok * P
                        mm = pe.transpose(wk[k // 2][:, at:at + P], xn[:, tok, k * P:k * P + P], ident)
                        if tok == 1:
                            mm.then_inc(norm_turned, 1)

            def wait_xnT(name):
                n = TURN[name]
                k = 8 if name == "moba" else 4
                extra = 4 if n > TURN["moba"] else 0
                pe.wait_ge(xnT_by_dve, 4 * n + extra + k)
                pe.wait_ge(xnT_by_act, 4 * n + extra + k)

            def gated_block(name, groups, before_down=None):
                c0, g0 = START[name], GROUP0[name]
                use = ACC[name]

                def gate_up(c, par_, turn=None):
                    for kind in range(2):
                        wait_chunk(c + kind, turn)
                        project(c + kind, xnT, wk[2 * kind + par_])

                def down(c, par_, g, first=False, last=False, turn=None):
                    wait_chunk(c, turn)
                    pe.wait_ge(hidden_ready, g0 + g + 1 if turn is None else turn * 2 + (g0 + g + 1))
                    w = rows_view(c)
                    for f in range(2):
                        for b in range(4):
                            if first and f == 0 and use:
                                pe.wait_ge(acc_read, 4 * (use - 1) + b + 1)
                            mm = pe.matmul(acc[b], hidT[:, par_, f, b // 2 * P:b // 2 * P + P],
                                           w[:, f, b % 2 * 512:b % 2 * 512 + 512],
                                           start=(first and f == 0), stop=(last and f == 1))
                            if last and f == 1 and b < 3:
                                mm.then_inc(acc_done, 1)
                    mm.then_inc(chunks_used, 1)

                gate_up(c0, 0)
                gate_up(c0 + 2, 1)
                if before_down:
                    before_down()
                down(c0 + 4, 0, 0, first=True)
                with pe.Fori(0, (groups - 2) // 2) as i:
                    for q in range(2):
                        gate_up(c0 + 5 + 3 * q, q, i)
                        down(c0 + 7 + 3 * q, 1 - q, 1 + q, turn=i)
                done = (groups - 2) // 2 * 2 + 2
                for j in range(done, groups):
                    c = c0 + 2 + 3 * (j - 1)
                    gate_up(c, j % 2)
                    down(c + 2, (j - 1) % 2, j - 1)
                down(c0 + 3 * groups - 1, (groups - 1) % 2, groups - 1, last=True)

            def rope(name, c0, n, xT, swap):
                base = ROPE0[name]

                def swapped(m):
                    pe.wait_ge(rope_raw, base + m + 1)
                    if base + m >= 2:
                        pe.wait_ge(rope_used, base + m - 1)
                    pe.matmul(wk[2 + m % 2], con_(swap), raw[:, m % 2, :], start=True, stop=True)\
                        .then_inc(rope_swapped, 1)

                for m in range(n):
                    wait_chunk(c0 + m)
                    project(c0 + m, xT, wk[m % 2])
                    if m:
                        swapped(m - 1)
                swapped(n - 1)

            def attention(a):
                def scores(u):
                    h, i = a.units[u]
                    if u >= 2:
                        pe.wait_ge(scores_read, a.base + u - 1)
                    w = P * (i + 1)
                    for g in range(a.groups):
                        at = 1024 * (u % 2) + g * w
                        mm = pe.matmul(wkf[:, at:at + w], a.q(h, g)[:, i * P:i * P + P], a.k(h, g)[:, 0:w],
                                       start=True, stop=True)
                    mm.then_inc(scores_ready, 1)

                def finish(u):
                    h, i = a.units[u]
                    pe.wait_ge(probs_ready, a.base + u + 1)
                    if u:
                        pe.wait_ge(probsT_ready, a.base + u)
                    n = a.width(i) // P
                    for b in range(n):
                        mm = pe.transpose(accf[:, b * P:b * P + P], prob[:, u % 2, b * P:b * P + P], ident)
                    mm.then_inc(probs_turned, 1)
                    pe.wait_ge(probsT_ready, a.base + u + 1)
                    if u >= 2:
                        pe.wait_ge(heads_read, a.base + u - 1)
                    row = 64 * (h % 2) if a.dh == 64 else 0
                    for b in range(n):
                        g, s = b // (i + 1), b % (i + 1)
                        mm = pe.matmul(acc[2 + u % 2][row:row + a.dh, 0:P], a.v(h, g, s), probT[:, b * P:b * P + P],
                                       start=(b == 0), stop=(b == n - 1))
                    mm.then_inc(heads_ready, 1)

                scores(0)
                for u in range(len(a.units)):
                    if u + 1 < len(a.units):
                        scores(u + 1)
                    finish(u)
                pe.wait_ge(heads_read, a.base + len(a.units))

            def s_ffn1():
                pe.wait_ge(tables_loaded, 32)
                norm("ffn1")
                wait_xnT("ffn1")
                gated_block("ffn1", FFN_GROUPS)

            def s_dil():
                norm("mix")
                wait_xnT("mix")
                rope("dil", START["dil_qk"], 6, xnT, "dil_swap")
                accumulate("dil_v", START["dil_v"], 4, lambda k: xnT[:, k, :], AQ)
                pe.wait_ge(rope_done, 6)
                pe.wait_ge(acc_read, 4 * (ACC["dil_v"] + 1))
                attention(dil)

            def shift_project(s, bank):
                if s >= 4:
                    pe.wait_ge(z_copied, s - 3)
                c = START["rkv"] + s - 2
                wait_chunk(c)
                project(c, xnT, bank)

            def s_rwkv_in():
                c = START["lora"]
                wait_chunk(c)
                project(c, xnT, wk[0])
                wait_chunk(c + 1)
                w = slot(c + 1)[:, 0:KT * 32].rearrange("p (k n) -> p k n", k=KT)
                for k in range(KT):
                    mm = pe.matmul(wk[1][0:32, 0:T], w[:, k, :], xnT[:, k, :], start=(k == 0), stop=(k == KT - 1))
                mm.then_inc(rest_ready, 1)
                wa, g2 = slot(c + 1)[:, KT * 32:KT * 32 + D], slot(c + 2)
                wait_chunk(c + 2)
                pe.wait_ge(lora_act, 3)
                for r in range(4):
                    wb, ab, gb = (wk[2], wk[3], acc[0]) if r % 2 == 0 else (acc[1], acc[2], acc[3])
                    if r >= 2:
                        pe.wait_ge(lora_by_act, r - 1)
                        pe.wait_ge(lora_by_dve, r - 1)
                    for f in range(2):
                        n = (2 * r + f) * P
                        pe.matmul(wb[:, f * T:f * T + T], wa[0:64, n:n + P], zlora[0:64, 0, :], start=True, stop=True)
                    for f in range(2):
                        n = (2 * r + f) * P
                        mm = pe.matmul(ab[:, f * T:f * T + T], wa[64:128, n:n + P], zlora[64:128, 0, :],
                                       start=True, stop=True)
                    if r == 3:
                        mm.then_inc(chunks_used, 1)
                    for f in range(2):
                        n = (2 * r + f) * P
                        pe.matmul(gb[:, f * T:f * T + T], g2[:, n:n + P], zlora[:, 1, :], start=True, stop=False)
                        mm = pe.matmul(gb[:, f * T:f * T + T], g2[0:32, D + n:D + n + P], zlora[0:32, 2, :],
                                       start=False, stop=True)
                    mm.then_inc(chunks_used if r == 3 else lora_done, 1)
                for s in range(2, 14):
                    if s == 2:
                        pe.wait_ge(lora_by_act, 3)
                        pe.wait_ge(lora_by_dve, 3)
                    shift_project(s, wk[s % 4])
                pe.wait_ge(kk_squared, 1)
                pe.wait_ge(z_copied, 14)
                for b in range(4):
                    mm = pe.matmul(wk[b], head_ones, A(7)[:, b * 512:b * 512 + 512], start=True, stop=True)
                mm.then_inc(kk_summed, 1)
                pe.wait_ge(lora_by_act, 4)
                pe.wait_ge(lora_by_dve, 4)
                pe.wait_ge(rk_done, 1)
                for b in range(4):
                    mm = pe.matmul(acc[b], head_ones, A(13)[:, b * 512:b * 512 + 512], start=True, stop=True)
                mm.then_inc(rk_summed, 1)
                pe.wait_ge(kk_root, 1)
                pe.wait_ge(z_shifted, 14)
                for c in range(2):
                    for p in range(PAIRS):
                        mm = pe.transpose(wkf[:, c * D + p * P:c * D + p * P + P], V8[:, p, c * P:c * P + P], ident)
                mm.then_inc(turned_vbk, 1)
                pe.wait_ge(bonus_done, 1)
                pe.wait_ge(tilde_done, 1)
                for n, src in enumerate((B8, KD8)):
                    for p in range(PAIRS):
                        mm = pe.transpose(accf[:, n * D + p * P:n * D + p * P + P], src[:, p, 0:P], ident)
                mm.then_inc(turned_vbk, 1)
                pe.wait_ge(v_tok, 1)
                pe.wait_ge(bk_tok, 1)

            def s_rwkv_solve():
                def unit(g, i):
                    h = 4 * (g % 4) + i
                    p, q, c = h // 2, h % 2, g // 4
                    return p, slice(64 * q, 64 * q + 64), c, slice(c * P, c * P + P), slice(64 * h, 64 * h + 64)

                def mm(out_, lhsT, rhs, start=True, stop=True):
                    return pe.matmul(out_, lhsT, rhs, start=start, stop=stop)

                for g in range(8):
                    for st in range(1, 11):
                        for i in range(4):
                            p, rows, c, ts, hc = unit(g, i)
                            a, b = wk[i], acc[i]
                            nd, na = lane_counts(g, st - 1)
                            if nd:
                                pe.wait_ge(lane_dve[i], nd)
                            if na:
                                pe.wait_ge(lane_act[i], na)
                            dT, tT, dd = (XD[i][:, n, :] for n in range(3))
                            n_, nT = NN[i][:, 0:P], NN[i][:, P:2 * P]
                            n2T, n2 = NN2[i][:, 0:P], NN2[i][:, P:2 * P]
                            if st == 1:
                                ar = AR[rows, 2 * p + c].rearrange("p s t -> p (s t)")
                                mm(a[:, 0:256], B8[rows, p, ts], ar)
                                mm(a[:, 256:512], KD8[rows, p, ts], ar)
                                last = mm(b[:, 0:P], AR[rows, 2 * p + c, 0, :], B8[rows, p, ts])
                            elif st == 2:
                                mm(a[:, 0:P], dd, dT)
                                mm(a[:, P:2 * P], dT, dd)
                                last = mm(a[:, 256:320], mbk[i][:, 256:384], Vtok[:, c, hc], stop=(c == 0))
                                if c:
                                    last = mm(a[:, 256:320], AR[rows, 2 * p + c, 0, :], state[rows, p, :], start=False)
                            elif st == 3:
                                mm(a[:, 0:P], dd, dT)
                                mm(a[:, P:2 * P], dT, dd)
                                last = mm(b[:, 0:P], dd, tT)
                            elif st == 4:
                                mm(a[:, 0:P], dT, dd)
                                last = mm(b[:, 0:P], dd, tT)
                            elif st == 5:
                                last = mm(b[:, 0:P], dd, tT)
                            elif st == 6:
                                mm(a[:, 0:P], tT, LO[i])
                                mm(a[:, P:2 * P], LO[i], tT)
                                last = mm(b[:, 0:64], tT, Wl[i])
                            elif st == 7:
                                mm(a[:, 0:P], n_, nT)
                                mm(a[:, P:2 * P], nT, n_)
                                last = mm(b[:, 0:64], nT, Ul[i])
                            elif st == 8:
                                mm(a[:, 0:P], n2, n2T)
                                last = mm(b[:, 0:64], n2T, Ul[i])
                            elif st == 9:
                                last = mm(b[:, 0:64], N4T[i], Ul[i])
                            else:
                                if c:
                                    mm(a[:, 0:64], AR[rows, 2 * p + c, 1, :], state[rows, p, :], stop=False)
                                mm(a[:, 0:64], mbk[i][:, 128:256], Ul[i], start=(c == 0), stop=False)
                                last = mm(a[:, 0:64], mbk[i][:, 384:512], Vtok[:, c, hc], start=False)
                                if c == 0:
                                    mm(b[rows, 0:64], BKtok[:, 0, hc], Ul[i], stop=False)
                                    last = mm(b[rows, 0:64], BKtok[:, 1, hc], Vtok[:, c, hc], start=False)
                            last.then_inc(lane_pe[i], 1)
                for i in range(4):
                    pe.wait_ge(lane_dve[i], lane_counts(7, 10)[0])
                    pe.wait_ge(lane_act[i], lane_counts(7, 10)[1])

            def s_mix_out():
                accumulate("gate_a", START["gate_a"], 4, lambda k: xnT[:, k, :])
                accumulate("gate_r", START["gate_r"], 4, lambda k: xnT[:, k, :])
                accumulate("attn_up", START["attn_up"], 1, lambda k: attT[:, k, :])
                pe.wait_ge(y_normed, 1)
                for p in range(PAIRS):
                    for c in range(2):
                        mm = pe.transpose(wk[p // 2][:, p % 2 * T + c * P:p % 2 * T + c * P + P],
                                          Ytok[:, c, p * P:p * P + P], ident)
                    if p % 2:
                        mm.then_inc(y_turned, 1)
                pe.wait_ge(z_done, 1)
                accumulate("rwkv_out", START["rwkv_out"], 4, lambda k: zT[:, k, :])
                pe.wait_ge(merge_done, 1)
                for k in range(KT):
                    for tok in range(NT):
                        mm = pe.transpose(wk[k // 2][:, k % 2 * T + tok * P:k % 2 * T + tok * P + P],
                                          merged[:, tok * D + k * P:tok * D + k * P + P], ident)
                    if k % 2:
                        mm.then_inc(merge_turned, 1)
                pe.wait_ge(merge_copied, 1)
                accumulate("mix_out", START["mix_out"], 4, lambda k: mergedT[:, k, :])

            def s_ffn2():
                norm("ffn2")
                wait_xnT("ffn2")
                gated_block("ffn2", FFN_GROUPS)

            def s_ret():
                norm("ret")
                wait_xnT("ret")
                for m in range(8):
                    if m >= 4:
                        pe.wait_ge(rot_read, m - 3)
                    wait_chunk(START["ret_qk"] + m)
                    project(START["ret_qk"] + m, xnT, wk[m % 4])
                for n in range(2):
                    accumulate(f"ret_v{n}", START["ret_v"] + 4 * n, 4, lambda k: xnT[:, k, :])
                pe.wait_ge(rot_done, 8)
                for h in range(RET_HEADS):
                    for s, t0, at in ((0, 0, 0), (1, P, T)):
                        for f in range(2):
                            mm = pe.matmul(wk[h][:, at:at + T - t0], ret_k[:, 2 * h + f, s * P:s * P + P],
                                           ret_q[:, 2 * h + f, t0:T], start=(f == 0), stop=(f == 1))
                    mm.then_inc(rs_ready, 1)
                for n in range(2):
                    accumulate(f"ret_g{n}", START["ret_g"] + 4 * n, 4, lambda k: xnT[:, k, :])

                def outputs(h):
                    pe.wait_ge(rs_masked, h + 1)
                    for tok in range(NT):
                        bank = acc[2 * (h % 2) + tok]
                        if h >= 2:
                            pe.wait_ge(ret_y_done, NT * (h - 2) + tok + 1)
                        elif h == 0:
                            pe.wait_ge(acc_read, 4 * ACC["ret_g1"] + 4)
                        v = ret_v[:, :, h * RET_DV:(h + 1) * RET_DV]
                        mm = pe.matmul(bank, ret_sT[:, h, tok * P:tok * P + P], v[:, 0, :], start=True, stop=(tok == 0))
                        if tok:
                            mm = pe.matmul(bank, ret_sT[:, h, T:T + P], v[:, 1, :], start=False, stop=True)
                        mm.then_inc(o_ready, 1)

                def turn(h):
                    pe.wait_ge(ret_y_done, NT * h + NT)
                    if h >= 2:
                        pe.wait_ge(ret_copied, h - 1)
                    for j in range(4):
                        for tok in range(NT):
                            at = 1024 * (h % 2) + j * T + tok * P
                            mm = pe.transpose(wkf[:, at:at + P], ret_y[:, tok, (4 * h + j) * P:(4 * h + j + 1) * P], ident)
                    mm.then_inc(ret_turned, 1)

                outputs(0)
                outputs(1)
                for h in range(RET_HEADS):
                    turn(h)
                    if h + 2 < RET_HEADS:
                        outputs(h + 2)
                pe.wait_ge(ret_copied, RET_HEADS)
                accumulate("ret_out", START["ret_out"], 8, lambda k: ret_yT[:, k, :])

            def s_moe(l):
                name = f"moe{l}"
                norm(name)
                wait_xnT(name)
                pe.wait_ge(acc_read, 4 * ACC[name])
                rw = par_(f"route_w{l}", KT * ROUTE).rearrange("p (k n) -> p k n", k=KT)
                for tok in range(NT):
                    for k in range(KT):
                        mm = pe.matmul(acc[tok][:, 0:ROUTE], xnT[:, k, tok * P:tok * P + P], rw[:, k, :],
                                       start=(k == 0), stop=(k == KT - 1))
                mm.then_inc(routed, 1)

                def spread_weights():
                    pe.wait_ge(combine_ready, l + 1)
                    for tok in range(NT):
                        mm = pe.transpose(acc[2][0:EXPERTS, tok * P:tok * P + P],
                                          scratch[:, tok * EXPERTS:tok * EXPERTS + EXPERTS], ident)
                    mm.then_inc(combine_turned, 1)
                    pe.wait_ge(weightT_ready, l + 1)
                    for half in range(2):
                        if half:
                            pe.wait_ge(spread_read, 2 * l + 1)
                        for e in range(8):
                            n = 8 * half + e
                            mm = pe.matmul(accf[:, e * T:e * T + T], ident[0:EXPERTS, n:n + 1].broadcast_to((EXPERTS, P)),
                                           weightT[0:EXPERTS, :], start=True, stop=True)
                        mm.then_inc(spread, 1)
                    pe.wait_ge(spread_read, 2 * l + 2)

                gated_block(name, MOE_GROUPS, spread_weights)

            def s_moba():
                norm("moba")
                wait_xnT("moba")
                rope("moba_k", START["moba_k"], 4, xnT, "moba_swap")
                accumulate("moba_v", START["moba_v"], 4, lambda k: xnT[:, k, :])
                rope("moba_q", START["moba_q"], 4, xqT, "moba_swap")
                pe.wait_ge(rope_done, 14)
                pe.wait_ge(acc_read, 4 * (ACC["moba_v"] + 1))
                attention(moba)
                accumulate("moba_out", START["moba_out"], 4, lambda k: moba_oT[:, k, :])

            def s_final():
                pass

            s_ffn1()
            s_dil()
            s_rwkv_in()
            s_rwkv_solve()
            s_mix_out()
            s_ffn2()
            s_ret()
            s_moe(0)
            s_moba()
            s_moe(1)
            s_final()

        @block.scalar
        def _(act):
            own = Steps(act, act_steps)
            act.dma_start(x[:, :, :], x_in.rearrange("(t p) d -> p t d", p=P)).then_inc(x_loaded, 16)
            act.dma_start(par[:, :], params).then_inc(tables_loaded, 16)
            act.dma_start(con[:, :], consts).then_inc(tables_loaded, 16)

            def norm(name, prev):
                n = NORM[name]
                if prev is None:
                    act.wait_ge(x_loaded, 16)
                elif prev == "mid":
                    act.wait_ge(x_scaled, 1)
                else:
                    act.wait_ge(acc_read, 4 * (ACC[prev] + 1))
                act.wait_ge(zeroed, 1)
                for tok in range(NT):
                    nc.scalar.activation(junk[:, tok, :], x[:, tok, :], ACT.Square, accum_out=ss[:, tok:tok + 1])\
                        .then_inc(norm_sum, 1)
                act.wait_ge(norm_sum, NT * (n + 1))
                nc.scalar.activation(std, ss, ACT.Sqrt, bias=small[:, 8:9], scale=1.0 / D).then_inc(norm_std, 1)

            def norm_gain(name, outs):
                n = TURN[name]
                for gain, dst in outs:
                    for k in (2, 3, 6, 7):
                        act.wait_ge(norm_turned, KT * n + (k | 1) + 1)
                        nc.scalar.activation(dst[:, k, :], wk[k // 2][:, k % 2 * T:k % 2 * T + T], ACT.Copy,
                                             scale=par_(gain)[:, k:k + 1]).then_inc(xnT_by_act, 1)

            def gated_block(name, groups, after_two=None):
                c0 = START[name]

                def silu(c, par_, turn=None):
                    act.wait_ge(chunks_used, c + 1 if turn is None else turn * 6 + (c + 1))
                    nc.scalar.activation(sil[:, par_].rearrange("p f t -> p (f t)"), wk[par_], ACT.Silu)\
                        .then_inc(silu_done, 1)

                silu(c0, 0)
                silu(c0 + 2, 1)
                if after_two:
                    after_two()
                with act.Fori(0, (groups - 2) // 2) as i:
                    for q in range(2):
                        silu(c0 + 5 + 3 * q, q, i)
                for j in range((groups - 2) // 2 * 2 + 2, groups):
                    silu(c0 + 2 + 3 * (j - 1), j % 2)

            def rope(name, c0, n):
                base = ROPE0[name]
                for m in range(n):
                    act.wait_ge(chunks_used, c0 + m + 1)
                    if base + m >= 2:
                        act.wait_ge(rope_used, base + m - 1)
                    nc.scalar.activation(raw[:, m % 2, :], wk[m % 2], ACT.Copy).then_inc(rope_raw, 1)

            def attention(a):
                def exps(u):
                    h, i = a.units[u]
                    act.wait_ge(bias_ready, a.base + u + 1)
                    s = prob[:, u % 2, 0:a.width(i)]
                    nc.scalar.activation(s, s, ACT.Exp, bias=small[:, 16 + u % 2:17 + u % 2], scale=a.scale,
                                         accum_out=small[:, 18 + u % 2:19 + u % 2]).then_inc(exp_done, 1)

                def evacuate(u):
                    h, i = a.units[u]
                    act.wait_ge(probs_turned, a.base + u + 1)
                    if u:
                        act.wait_ge(heads_ready, a.base + u)
                    nc.scalar.activation(probT[:, 0:a.width(i)], accf[:, 0:a.width(i)], ACT.Copy)\
                        .then_inc(probsT_ready, 1)

                exps(0)
                for u in range(len(a.units)):
                    if u + 1 < len(a.units):
                        exps(u + 1)
                    evacuate(u)

            def s_ffn1():
                norm("ffn1", None)
                act.wait_ge(tables_loaded, 32)
                norm_gain("ffn1", [("ffn1_norm", xnT)])
                gated_block("ffn1", FFN_GROUPS)

            def s_dil():
                norm("mix", "ffn1")
                norm_gain("mix", [("mix_norm", xnT)])
                rope("dil", START["dil_qk"], 6)
                attention(dil)

            def s_rwkv_in():
                def raw_z(s, bank, rows=P, f=2):
                    if s >= 2:
                        act.wait_ge(z_shifted, s - 1)
                    nc.scalar.activation(zraw[0:rows, s % 2, 0:f, 1:T + 1],
                                         bank[0:rows, 0:f * T].rearrange("p (f t) -> p f t", f=f), ACT.Copy)\
                        .then_inc(z_copied, 1)

                act.wait_ge(zeroed, 2)
                act.wait_ge(chunks_used, START["lora"] + 1)
                raw_z(0, wk[0])
                act.wait_ge(rest_ready, 1)
                raw_z(1, wk[1], 32, 1)
                act.wait_ge(z_shifted, 2)
                nc.scalar.activation(zlora[0:64, 0, :], zlora[0:64, 0, :], ACT.Tanh).then_inc(lora_act, 1)
                nc.scalar.activation(zlora[:, 1, :], zlora[:, 1, :], ACT.Sigmoid).then_inc(lora_act, 1)
                nc.scalar.activation(zlora[0:32, 2, :], zlora[0:32, 2, :], ACT.Sigmoid).then_inc(lora_act, 1)
                for r in range(4):
                    wb, ab = (wk[2], wk[3]) if r % 2 == 0 else (acc[1], acc[2])
                    if r < 3:
                        act.wait_ge(lora_done, r + 1)
                    else:
                        act.wait_ge(chunks_used, START["rkv"])
                    for f in range(2):
                        p = 2 * r + f
                        nc.scalar.activation(C8[:, p, :], wb[:, f * T:f * T + T], ACT.Sigmoid,
                                             bias=par_("rwkv_w0")[:, p:p + 1])
                        ins = nc.scalar.activation(A8[:, p, :], ab[:, f * T:f * T + T], ACT.Sigmoid,
                                                   bias=par_("rwkv_a0")[:, p:p + 1])
                    ins.then_inc(lora_by_act, 1)
                for s in range(2, 14):
                    act.wait_ge(chunks_used, START["rkv"] + s - 1)
                    raw_z(s, wk[s % 4])
                    if s == 11:
                        act.wait_ge(kk_scaled, 1)
                        nc.scalar.activation(A(7), A(3), ACT.Square).then_inc(kk_squared, 1)
                act.wait_ge(kk_summed, 1)
                nc.scalar.activation(A(6), wkf, ACT.Sqrt).then_inc(kk_root, 1)
                act.wait_ge(turned_vbk, 1)
                act.wait_ge(cum_done, 1)
                act.wait_ge(kk_done, 1)
                nc.scalar.activation(endf, endf, ACT.Exp, scale=-DECAY)
                nc.scalar.activation(startf, startf, ACT.Exp, scale=DECAY)
                nc.scalar.activation(A(6), A(5), ACT.Exp, scale=-DECAY)
                nc.scalar.activation(A(7), A(5), ACT.Exp, scale=DECAY).then_inc(decays_done, 1)
                act.wait_ge(decays_done, 1)
                nc.scalar.activation(A(5), wkf, ACT.Copy).then_inc(v_tok, 1)
                act.wait_ge(turned_vbk, 2)
                nc.scalar.activation(A(6), accf, ACT.Copy).then_inc(bk_tok, 1)

            def s_rwkv_solve():
                for g in range(8):
                    for st in range(2, 11):
                        if st in (5, 9):
                            continue
                        for i in range(4):
                            h, c = 4 * (g % 4) + i, g // 4
                            act.wait_ge(lane_pe[i], 10 * g + st)
                            a = wk[i]
                            two = a[:, 0:256].rearrange("p (n t) -> p n t", n=2)
                            if st == 2:
                                nc.scalar.activation(XD[i][:, 0::2, :], two, ACT.Copy)
                                ins = nc.scalar.activation(Wl[i], a[:, 256:320], ACT.Copy)
                            elif st == 3:
                                ins = nc.scalar.activation(XD[i][:, 0::2, :], two, ACT.Copy)
                            elif st == 4:
                                ins = nc.scalar.activation(XD[i][:, 2, :], a[:, 0:P], ACT.Copy)
                            elif st == 6:
                                ins = nc.scalar.activation(NN[i], a[:, 0:256], ACT.Copy)
                            elif st == 7:
                                ins = nc.scalar.activation(NN2[i], a[:, 0:256], ACT.Copy)
                            elif st == 8:
                                ins = nc.scalar.activation(N4T[i], a[:, 0:P], ACT.Copy)
                            else:
                                ins = nc.scalar.activation(Ytok[:, c, 64 * h:64 * h + 64], a[:, 0:64], ACT.Copy)
                            ins.then_inc(lane_act[i], 1)

            def s_mix_out():
                for i in range(4):
                    act.wait_ge(lane_pe[i], 80)
                act.dma_start(gbias, gate_bias.broadcast_to((P, 2 * D))).then_inc(bias_loaded, 16)
                act.wait_ge(y_centred, 1)
                nc.scalar.activation(A(0), A(7), ACT.Square).then_inc(y_squared, 1)
                act.wait_ge(y_var, 1)
                nc.scalar.activation(gvar, gvar, ACT.Sqrt, bias=small[:, 9:10], scale=1.0 / RW_N).then_inc(y_std, 1)
                for n, gate in enumerate((gate_a, gate_r)):
                    act.wait_ge(acc_read, 4 * (ACC["gate_a"] + n + 1))
                    nc.scalar.activation(gate, gate, ACT.Sigmoid).then_inc(gate_done, 1)
                for p in range(PAIRS):
                    act.wait_ge(y_turned, p // 2 + 1)
                    nc.scalar.activation(zT[:, p, :], wk[p // 2][:, p % 2 * T:p % 2 * T + T], ACT.Identity,
                                         bias=par_("rwkv_ln_b")[:, p:p + 1], scale=par_("rwkv_ln_w")[:, p:p + 1])\
                        .then_inc(y_affine, 1)
                act.wait_ge(merge_turned, 4)
                nc.scalar.activation(A(3), wkf, ACT.Copy).then_inc(merge_copied, 1)

            def s_ffn2():
                norm("ffn2", "mix_out")
                act.dma_start(gain_row, gains[0:1, :].broadcast_to((P, D))).then_inc(gain_loaded, 16)
                norm_gain("ffn2", [("ffn2_norm", xnT)])
                gated_block("ffn2", FFN_GROUPS)

            def s_ret():
                norm("mid", "ffn2")
                norm("ret", "mid")
                norm_gain("ret", [("ret_norm_2", xnT)])
                for n in range(2):
                    for b in range(4):
                        if b < 3:
                            act.wait_ge(acc_done, 3 * ACC[f"ret_g{n}"] + b + 1)
                        else:
                            act.wait_ge(chunks_used, START["ret_g"] + 4 * n + 4)
                        at = n * D + b % 2 * 512
                        nc.scalar.activation(ret_g[:, b // 2, at:at + 512], acc[b], ACT.Silu).then_inc(acc_read, 1)

                def sums(h):
                    for tok in range(NT):
                        u = NT * h + tok
                        act.wait_ge(o_ready, u + 1)
                        nc.scalar.activation(A(12)[:, tok * 512:tok * 512 + 512], acc[2 * (h % 2) + tok], ACT.Square,
                                             accum_out=ret_ss[:, u:u + 1]).then_inc(o_summed, 1)
                    act.wait_ge(o_summed, NT * h + NT)
                    nc.scalar.activation(ret_std[:, NT * h:NT * h + NT], ret_ss[:, NT * h:NT * h + NT], ACT.Sqrt,
                                         bias=small[:, 8:9], scale=1.0 / RET_DV).then_inc(o_std, 1)

                def copy(h):
                    act.wait_ge(ret_turned, h + 1)
                    nc.scalar.activation(ret_yT[:, 4 * h:4 * h + 4, :].rearrange("p k t -> p (k t)"),
                                         wkf[:, 1024 * (h % 2):1024 * (h % 2) + 1024], ACT.Copy).then_inc(ret_copied, 1)

                sums(0)
                sums(1)
                for h in range(RET_HEADS):
                    copy(h)
                    if h + 2 < RET_HEADS:
                        sums(h + 2)

            def s_moe(l):
                name = f"moe{l}"
                norm(name, ("ret_out", "moba_out")[l])
                norm_gain(name, [(f"ffn_norm_{l}", xnT)])
                act.wait_ge(route_shifted, l + 1)
                e4, e1 = scratch[:, 100:108], scratch[:, 150:152]
                nc.scalar.activation(e4, e4, ACT.Exp).then_inc(route_exp, 1)
                act.wait_ge(route_diff, l + 1)
                nc.scalar.activation(e1, e1, ACT.Exp).then_inc(route_exp2, 1)

                def spread_copies():
                    for half in range(2):
                        act.wait_ge(spread, 2 * l + half + 1)
                        nc.scalar.activation(A(8 + half), accf, ACT.Copy).then_inc(spread_read, 1)

                gated_block(name, MOE_GROUPS, spread_copies)

            def s_moba():
                norm("moba", "moe0")
                norm_gain("moba", [("kv_norm_2", xnT), ("attn_norm_2", xqT)])
                rope("moba_k", START["moba_k"], 4)
                rope("moba_q", START["moba_q"], 4)
                attention(moba)

            def s_final():
                act.dma_start(gain_row, gains[1:2, :].broadcast_to((P, D))).then_inc(gain_loaded, 16)
                norm("final", "moe1")
                act.wait_ge(stored_ready, 1)
                act.dma_start(out.rearrange("(t p) d -> p t d", p=P), final_out).then_inc(stored, 16)
                act.wait_ge(stored, 16)

            s_ffn1()
            s_dil()
            s_rwkv_in()
            s_rwkv_solve()
            s_mix_out()
            s_ffn2()
            s_ret()
            s_moe(0)
            s_moba()
            s_moe(1)
            s_final()

        @block.vector
        def _(dve):
            own = Steps(dve, dve_steps)
            nc.vector.memset(ones[:, :], 1.0)
            nc.vector.memset(small[:, 9:10], 64e-5)
            for n in range(4):
                nc.vector.memset(small[:, 12 + n:13 + n], 4.0 - n)
            nc.vector.memset(small[:, 8:9], EPS).then_inc(zeroed, 1)

            def norm(name):
                n = NORM[name]
                dve.wait_ge(norm_std, n + 1)
                own.did(nc.vector.reciprocal(rstd, std))
                own.settle()
                for tok in range(NT):
                    nc.vector.tensor_scalar(xn[:, tok, :], x[:, tok, :], rstd[:, tok:tok + 1], None, ALU.mult)\
                        .then_inc(norm_scaled, 1)

            def norm_gain(name, outs):
                n = TURN[name]
                for gain, dst in outs:
                    for k in (0, 1, 4, 5):
                        dve.wait_ge(norm_turned, KT * n + (k | 1) + 1)
                        nc.vector.tensor_scalar(dst[:, k, :], wk[k // 2][:, k % 2 * T:k % 2 * T + T],
                                                par_(gain)[:, k:k + 1], None, ALU.mult).then_inc(xnT_by_dve, 1)

            def wait_acc(name, last_chunk, b):
                if b < 3:
                    dve.wait_ge(acc_done, 3 * ACC[name] + b + 1)
                else:
                    dve.wait_ge(chunks_used, last_chunk + 1)

            def add_to_x(name, last_chunk, scale):
                for b in range(4):
                    wait_acc(name, last_chunk, b)
                    part = x[:, b // 2, b % 2 * 512:b % 2 * 512 + 512]
                    nc.vector.scalar_tensor_tensor(out=part, in0=acc[b], scalar=scale, in1=part, op0=ALU.mult,
                                                   op1=ALU.add).then_inc(acc_read, 1)

            def gated_block(name, groups, scale, weight=None):
                c0, g0 = START[name], GROUP0[name]

                def hidden(c, par_, g, turn=None):
                    dve.wait_ge(chunks_used, c + 1 if turn is None else turn * 6 + (c + 1))
                    dve.wait_ge(silu_done, g0 + g + 1 if turn is None else turn * 2 + (g0 + g + 1))
                    out_ = hidT[:, par_].rearrange("p f t -> p (f t)")
                    mul = nc.vector.tensor_tensor(out_, sil[:, par_].rearrange("p f t -> p (f t)"), wk[2 + par_],
                                                  ALU.mult)
                    if weight is None:
                        mul.then_inc(hidden_ready, 1)
                        return
                    mul.then_inc(gated, 1)
                    n = weight + g + 1
                    dve.wait_ge(gated, n if turn is None else turn * 2 + n)
                    we = by_expert[:, g // 2:g // 2 + 1, :] if turn is None else by_expert[:, bass.ds(turn + g // 2, 1), :]
                    nc.vector.tensor_tensor(hidT[:, par_], hidT[:, par_], we.broadcast_to((P, 2, T)), ALU.mult)\
                        .then_inc(hidden_ready, 1)

                hidden(c0 + 1, 0, 0)
                hidden(c0 + 3, 1, 1)
                with dve.Fori(0, (groups - 2) // 2) as i:
                    for q in range(2):
                        hidden(c0 + 6 + 3 * q, q, 2 + q, i)
                for j in range((groups - 2) // 2 * 2 + 2, groups):
                    hidden(c0 + 3 + 3 * (j - 1), j % 2, j)
                add_to_x(name, c0 + 3 * groups - 1, scale)

            def rope(name, n, dst, cos, sin):
                base = ROPE0[name]
                cs, sn = (con_(t).unsqueeze(1).broadcast_to((P, 2, T)) for t in (cos, sin))
                for m in range(n):
                    dve.wait_ge(rope_raw, base + m + 1)
                    r = raw[:, m % 2, :].rearrange("p (f t) -> p f t", f=2)
                    d = dst[:, 2 * m:2 * m + 2, :]
                    tmp = turned[:, m % 2, :].rearrange("p (f t) -> p f t", f=2)
                    own.did(nc.vector.tensor_tensor(d, r, cs, ALU.mult))
                    dve.wait_ge(rope_swapped, base + m + 1)
                    nc.vector.tensor_tensor(tmp, wk[2 + m % 2].rearrange("p (f t) -> p f t", f=2), sn, ALU.mult)\
                        .then_inc(rope_used, 1)
                    own.settle()
                    dve.wait_ge(rope_used, base + m + 1)
                    nc.vector.tensor_tensor(d, d, tmp, ALU.add).then_inc(rope_done, 1)

            def attention(a):
                def masked(u):
                    h, i = a.units[u]
                    w = a.width(i)
                    dve.wait_ge(scores_ready, a.base + u + 1)
                    if u >= 2:
                        dve.wait_ge(probs_turned, a.base + u - 1)
                    s = prob[:, u % 2, 0:w]
                    nc.vector.tensor_tensor(s, wkf[:, 1024 * (u % 2):1024 * (u % 2) + w], con_(a.mask[i]), ALU.add)\
                        .then_inc(scores_read, 1)
                    dve.wait_ge(scores_read, a.base + u + 1)
                    mx = small[:, 20 + u % 2:21 + u % 2]
                    own.did(nc.vector.tensor_reduce(mx, s, AX.X, ALU.max))
                    own.settle()
                    nc.vector.tensor_scalar(small[:, 16 + u % 2:17 + u % 2], mx, -a.scale, None, ALU.mult)\
                        .then_inc(bias_ready, 1)

                def normalised(u):
                    h, i = a.units[u]
                    dve.wait_ge(exp_done, a.base + u + 1)
                    rl = small[:, 22 + u % 2:23 + u % 2]
                    own.did(nc.vector.reciprocal(rl, small[:, 18 + u % 2:19 + u % 2]))
                    own.settle()
                    s = prob[:, u % 2, 0:a.width(i)]
                    nc.vector.tensor_scalar(s, s, rl, None, ALU.mult).then_inc(probs_ready, 1)

                def evacuate(u):
                    h, i = a.units[u]
                    row = 64 * (h % 2) if a.dh == 64 else 0
                    dve.wait_ge(heads_ready, a.base + u + 1)
                    nc.vector.tensor_copy(a.outT(h, i), acc[2 + u % 2][row:row + a.dh, 0:P]).then_inc(heads_read, 1)

                masked(0)
                for u in range(len(a.units)):
                    if u + 1 < len(a.units):
                        masked(u + 1)
                    normalised(u)
                    if u:
                        evacuate(u - 1)
                evacuate(len(a.units) - 1)

            def s_ffn1():
                norm("ffn1")
                dve.wait_ge(tables_loaded, 32)
                norm_gain("ffn1", [("ffn1_norm", xnT)])
                gated_block("ffn1", FFN_GROUPS, 0.5)

            def s_dil():
                norm("mix")
                norm_gain("mix", [("mix_norm", xnT)])
                rope("dil", 6, dil_qk, "dil_cos", "dil_sin")
                for b in range(4):
                    wait_acc("dil_v", START["dil_v"] + 3, b)
                    n0 = b % 2 * 512
                    n1 = min(n0 + 512, AQ)
                    nc.vector.tensor_copy(dil_v[:, b // 2, n0:n1], acc[b][:, 0:n1 - n0]).then_inc(acc_read, 1)
                attention(dil)

            def s_rwkv_in():
                nc.vector.memset(zraw[:, :, :, 0:1], 0.0).then_inc(zeroed, 1)
                dve.wait_ge(zeroed, 2)

                def shift(s, outs, mus, rows=P):
                    f = len(outs)
                    dve.wait_ge(z_copied, s + 1)
                    cur, prev = zraw[0:rows, s % 2, 0:f, 1:T + 1], zraw[0:rows, s % 2, 0:f, 0:T]
                    diff = shifted[0:rows, 0:f, :]
                    own.did(nc.vector.tensor_tensor(diff, prev, cur, ALU.subtract))
                    own.settle()
                    for j in range(f):
                        ins = nc.vector.scalar_tensor_tensor(out=outs[j], in0=diff[:, j, :],
                                                             scalar=par_("mu", 27)[0:rows, mus[j]:mus[j] + 1],
                                                             in1=cur[:, j, :], op0=ALU.mult, op1=ALU.add)
                    ins.then_inc(z_shifted, 1)
                    dve.wait_ge(z_shifted, s + 1)

                def bc(name):
                    return par_(name).unsqueeze(2).broadcast_to((P, PAIRS, T))

                def op(ins):
                    own.did(ins)
                    own.settle()

                TT, STT = nc.vector.tensor_tensor, nc.vector.scalar_tensor_tensor
                shift(0, [zlora[:, 0, :], zlora[:, 1, :]], [24, 25])
                shift(1, [zlora[0:32, 2, :]], [26], 32)
                for r in range(4):
                    gb = acc[0] if r % 2 == 0 else acc[3]
                    if r < 3:
                        dve.wait_ge(lora_done, r + 1)
                    else:
                        dve.wait_ge(chunks_used, START["rkv"])
                    nc.vector.tensor_copy(G8[:, 2 * r:2 * r + 2, :], gb.rearrange("p (f t) -> p f t", f=2))\
                        .then_inc(lora_by_dve, 1)

                def shift_rkv(s):
                    dst = (R8, K8, V8)[(s - 2) // 4]
                    n = (s - 2) % 4 * 2
                    shift(s, [dst[:, n, :], dst[:, n + 1, :]], [2 * (s - 2), 2 * (s - 2) + 1])

                for s in range(2, 10):
                    shift_rkv(s)
                nc.vector.tensor_tensor(KK8, K8, bc("rwkv_k_k"), ALU.mult).then_inc(kk_scaled, 1)
                for s in range(10, 14):
                    shift_rkv(s)
                dve.wait_ge(lora_by_act, 4)
                C = by_chunk(5)
                for n in range(2 * PAIRS):
                    ins = nc.vector.tensor_tensor_scan(C[:, n, :], ones[:, :], C[:, n, :], 0.0, ALU.mult, ALU.add)
                op(ins)
                nc.vector.tensor_copy(mid, C[:, :, 63])
                op(nc.vector.tensor_copy(startf, C[:, :, 63]))
                midc = mid.rearrange("p (k c) -> p k c", c=2)
                last = C.rearrange("p (k c) t -> p k c t", c=2)[:, :, 0, P - 1]
                op(TT(endf, last, midc[:, :, 0], ALU.subtract))
                op(TT(endf, endf, midc[:, :, 1], ALU.add))
                TT(C, C, mid.unsqueeze(2).broadcast_to((P, 2 * PAIRS, P)), ALU.subtract).then_inc(cum_done, 1)
                op(STT(out=BON, in0=A8, scalar=-1.0, in1=bc("rwkv_k_a"), op0=ALU.add, op1=ALU.mult))
                op(STT(out=K8, in0=BON, scalar=1.0, in1=K8, op0=ALU.add, op1=ALU.mult))
                op(TT(BON, R8, K8, ALU.mult))
                TT(BON, BON, bc("rwkv_r_k"), ALU.mult).then_inc(rk_done, 1)
                dve.wait_ge(kk_root, 1)
                nr = A(6)
                op(nc.vector.tensor_scalar(nr, nr, 1e-12, None, ALU.max))
                op(nc.vector.reciprocal(nr, nr))
                TT(A(3), A(3), nr, ALU.mult).then_inc(kk_done, 1)
                dve.wait_ge(kk_done, 1)
                op(TT(A(4), A(3), A(4), ALU.mult))
                dve.wait_ge(rk_summed, 1)
                TT(A(13), accf, A(2), ALU.mult).then_inc(bonus_done, 1)
                dve.wait_ge(decays_done, 1)
                e1, kkc = by_chunk(6), by_chunk(3)
                TT(AR[:, :, 1, :], by_chunk(0), e1, ALU.mult)
                STT(out=AR[:, :, 0, 1:P], in0=kkc[:, :, 1:P], scalar=-1.0, in1=e1[:, :, 0:P - 1], op0=ALU.mult,
                    op1=ALU.mult)
                STT(out=AR[:, :, 0, 0], in0=kkc[:, :, 0], scalar=-1.0, in1=startf, op0=ALU.mult, op1=ALU.mult)
                TT(A(10), A(4), A(7), ALU.mult)
                TT(A(11), A(1), A(7), ALU.mult).then_inc(tilde_done, 1)

            def s_rwkv_solve():
                dve.wait_ge(tilde_done, 1)
                dve.wait_ge(turned_vbk, 1)
                up2 = con_("tri_up").unsqueeze(1).broadcast_to((P, 2, 256))
                for g in range(8):
                    for st in (1, 3, 4, 5, 6, 7, 8, 9, 10):
                        if st == 10 and g >= 4:
                            continue
                        for i in range(4):
                            h, c = 4 * (g % 4) + i, g // 4
                            dve.wait_ge(lane_pe[i], 10 * g + st)
                            a, b = wk[i], acc[i]
                            if st == 1:
                                own.did(nc.vector.tensor_tensor(XD[i][:, 0, :], a[:, 0:P], con_("blk_up"), ALU.mult))
                                nc.vector.tensor_tensor(mbk[i].rearrange("p (n t) -> p n t", n=2),
                                                        a.rearrange("p (n t) -> p n t", n=2), up2, ALU.mult)
                                nc.vector.tensor_tensor(XD[i][:, 2, :], b[:, 0:P], con_("blk_low"), ALU.mult)
                                nc.vector.tensor_tensor(LO[i], b[:, 0:P], con_("off_low"), ALU.mult)
                                own.settle()
                                ins = nc.vector.tensor_tensor(XD[i][:, 1, :], XD[i][:, 0, :], ident, ALU.add)
                            elif st in (3, 4, 5):
                                ins = nc.vector.tensor_tensor(XD[i][:, 1, :], XD[i][:, 1, :], b[:, 0:P], ALU.add)
                            elif st == 6:
                                ins = nc.vector.tensor_copy(Ul[i], b[:, 0:64])
                            elif st in (7, 8, 9):
                                ins = nc.vector.tensor_tensor(Ul[i], Ul[i], b[:, 0:64], ALU.add)
                            else:
                                rows = slice(64 * (h % 2), 64 * (h % 2) + 64)
                                ins = nc.vector.tensor_scalar(state[rows, h // 2, :], b[rows, 0:64],
                                                              endf[rows, h // 2:h // 2 + 1], None, ALU.mult)
                            ins.then_inc(lane_dve[i], 1)

            def s_mix_out():
                def op(ins):
                    own.did(ins)
                    own.settle()

                for i in range(4):
                    dve.wait_ge(lane_act[i], lane_counts(7, 10)[1])
                Y = A(7).rearrange("p (h n) -> p h n", n=RW_N)
                shape = (P, 2 * RW_HEADS, RW_N)
                op(nc.vector.tensor_reduce(gsum, Y, AX.X, ALU.add))
                op(nc.vector.tensor_scalar(gsum, gsum, 1.0 / RW_N, None, ALU.mult))
                nc.vector.tensor_tensor(Y, Y, gsum.unsqueeze(2).broadcast_to(shape), ALU.subtract).then_inc(y_centred, 1)
                dve.wait_ge(y_squared, 1)
                nc.vector.tensor_reduce(gvar, A(0).rearrange("p (h n) -> p h n", n=RW_N), AX.X, ALU.add)\
                    .then_inc(y_var, 1)
                dve.wait_ge(y_std, 1)
                op(nc.vector.reciprocal(gvar, gvar))
                nc.vector.tensor_tensor(Y, Y, gvar.unsqueeze(2).broadcast_to(shape), ALU.mult).then_inc(y_normed, 1)
                dve.wait_ge(bias_loaded, 16)
                for n, (name, gate) in enumerate((("gate_a", gate_a), ("gate_r", gate_r))):
                    for b in range(4):
                        wait_acc(name, START[name] + 3, b)
                        at = b // 2 * D + b % 2 * 512
                        nc.vector.tensor_tensor(gate[:, at:at + 512], acc[b],
                                                gbias[:, n * D + b % 2 * 512:n * D + b % 2 * 512 + 512], ALU.add)\
                            .then_inc(acc_read, 1)
                dve.wait_ge(gate_done, 1)
                for b in range(4):
                    wait_acc("attn_up", START["attn_up"], b)
                    at = b // 2 * D + b % 2 * 512
                    nc.vector.tensor_tensor(merged[:, at:at + 512], acc[b], gate_a[:, at:at + 512], ALU.mult)\
                        .then_inc(acc_read, 1)
                dve.wait_ge(y_affine, PAIRS)
                op(nc.vector.tensor_tensor(A(1), A(1), A(13), ALU.add))
                nc.vector.tensor_tensor(A(1), A(1), A(12), ALU.mult).then_inc(z_done, 1)
                dve.wait_ge(gate_done, 2)
                for b in range(4):
                    wait_acc("rwkv_out", START["rwkv_out"] + 3, b)
                    at = b // 2 * D + b % 2 * 512
                    nc.vector.tensor_tensor(mpart[:, at:at + 512], acc[b], gate_r[:, at:at + 512], ALU.mult)\
                        .then_inc(acc_read, 1)
                dve.wait_ge(acc_read, 4 * ACC["rwkv_out"] + 4)
                nc.vector.tensor_tensor(merged, merged, mpart, ALU.add).then_inc(merge_done, 1)
                add_to_x("mix_out", START["mix_out"] + 3, 1.0)

            def s_ffn2():
                norm("ffn2")
                norm_gain("ffn2", [("ffn2_norm", xnT)])
                gated_block("ffn2", FFN_GROUPS, 0.5)

            def s_ret():
                norm("mid")
                dve.wait_ge(norm_scaled, NT * (NORM["mid"] + 1))
                dve.wait_ge(gain_loaded, 16)
                nc.vector.tensor_tensor(x[:, :, :], xn, gain_row.unsqueeze(1).broadcast_to((P, NT, D)), ALU.mult)\
                    .then_inc(x_scaled, 1)
                norm("ret")
                norm_gain("ret", [("ret_norm_2", xnT)])
                cs, sn = (con_(n).unsqueeze(1).broadcast_to((P, 2, T)) for n in ("ret_cos", "ret_sin"))
                for m in range(8):
                    dve.wait_ge(chunks_used, START["ret_qk"] + m + 1)
                    bank = wk[m % 4].rearrange("p (f t) -> p f t", f=2)
                    q = m % 2
                    c_, s_ = ret_tmp[:, 2 * q], ret_tmp[:, 2 * q + 1]
                    dst = (ret_q if m < 4 else ret_k)[:, m % 4 * 2:m % 4 * 2 + 2, :]
                    nc.vector.tensor_tensor(c_, bank, cs, ALU.mult)
                    nc.vector.tensor_tensor(s_, bank, sn, ALU.mult).then_inc(rot_read, 1)
                    dve.wait_ge(rot_read, m + 1)
                    nc.vector.tensor_tensor(dst[:, 0, :], c_[:, 0, :], s_[:, 1, :], ALU.subtract)
                    nc.vector.tensor_tensor(dst[:, 1, :], s_[:, 0, :], c_[:, 1, :], ALU.add).then_inc(rot_done, 1)
                for n in range(2):
                    for b in range(4):
                        wait_acc(f"ret_v{n}", START["ret_v"] + 4 * n + 3, b)
                        at = n * D + b % 2 * 512
                        nc.vector.tensor_copy(ret_v[:, b // 2, at:at + 512], acc[b]).then_inc(acc_read, 1)
                for h in range(RET_HEADS):
                    dve.wait_ge(rs_ready, h + 1)
                    nc.vector.tensor_tensor(ret_sT[:, h, :], wk[h][:, 0:384],
                                            con_("ret_decay")[:, h * 384:h * 384 + 384], ALU.mult).then_inc(rs_masked, 1)
                for h in range(RET_HEADS):
                    dve.wait_ge(o_std, h + 1)
                    dve.wait_ge(acc_read, 4 * ACC["ret_g1"] + 4)
                    own.did(nc.vector.reciprocal(ret_std[:, NT * h:NT * h + NT], ret_std[:, NT * h:NT * h + NT]))
                    own.settle()
                    for tok in range(NT):
                        u = NT * h + tok
                        at = slice(h * RET_DV, (h + 1) * RET_DV)
                        nc.vector.scalar_tensor_tensor(out=ret_y[:, tok, at], in0=acc[2 * (h % 2) + tok],
                                                       scalar=ret_std[:, u:u + 1], in1=ret_g[:, tok, at],
                                                       op0=ALU.mult, op1=ALU.mult).then_inc(ret_y_done, 1)
                add_to_x("ret_out", START["ret_out"] + 7, 1.0)

            def s_moe(l):
                name = f"moe{l}"
                norm(name)
                norm_gain(name, [(f"ffn_norm_{l}", xnT)])

                def op(ins):
                    own.did(ins)
                    own.settle()

                def take(at, *shape):
                    flat = scratch[:, at:at + int(np.prod(shape))]
                    names = "abc"[:len(shape)]
                    return flat.rearrange(f"p ({' '.join(names)}) -> p {' '.join(names)}", **dict(zip(names, shape)))

                def wide(t, n):
                    return t.unsqueeze(2).broadcast_to((P, NT, n))

                TT = nc.vector.tensor_tensor
                logits = take(40, NT, ROUTE)
                dve.wait_ge(routed, l + 1)
                op(TT(logits, ps[:, 4:6, 0:ROUTE],
                      par_(f"route_b{l}", ROUTE).unsqueeze(1).broadcast_to((P, NT, ROUTE)), ALU.add))
                prob4, first, score, sel, sel2 = (take(a, NT, 4) for a in (100, 110, 120, 130, 140))
                e1, top, total, w1, val = (scratch[:, a:a + NT] for a in (150, 152, 154, 156, 158))
                oh1, oh2, parts = take(160, NT, 4), take(170, NT, 4), take(180, NT, 4, 4)
                ramp = small[:, 12:16].unsqueeze(1).broadcast_to((P, NT, 4))

                def first_max(src, onehot, best):
                    op(nc.vector.tensor_reduce(best, src, AX.X, ALU.max))
                    op(TT(onehot, src, wide(best, 4), ALU.is_equal))
                    op(TT(score, onehot, ramp, ALU.mult))
                    op(nc.vector.tensor_reduce(total, score, AX.X, ALU.max))
                    op(TT(onehot, score, wide(total, 4), ALU.is_equal))

                op(nc.vector.tensor_reduce(top, logits[:, :, 0:4], AX.X, ALU.max))
                TT(prob4, logits[:, :, 0:4], wide(top, 4), ALU.subtract).then_inc(route_shifted, 1)
                dve.wait_ge(route_exp, l + 1)
                op(nc.vector.tensor_reduce(total, prob4, AX.X, ALU.add))
                op(nc.vector.reciprocal(total, total))
                op(TT(prob4, prob4, wide(total, 4), ALU.mult))
                first_max(prob4, first, val)
                op(TT(parts, logits[:, :, 4:20].rearrange("p t (g e) -> p t g e", g=4),
                      first.unsqueeze(3).broadcast_to((P, NT, 4, 4)), ALU.mult))
                op(nc.vector.tensor_reduce(sel, parts.rearrange("p t g e -> p t e g"), AX.X, ALU.add))
                first_max(sel, oh1, top)
                op(nc.vector.scalar_tensor_tensor(out=sel2, in0=oh1, scalar=MASKED, in1=sel, op0=ALU.mult, op1=ALU.add))
                first_max(sel2, oh2, w1)
                TT(e1, w1, top, ALU.subtract).then_inc(route_diff, 1)
                dve.wait_ge(route_exp2, l + 1)
                op(nc.vector.tensor_scalar(w1, e1, 1.0, None, ALU.add))
                op(nc.vector.reciprocal(w1, w1))
                op(TT(w1, w1, val, ALU.mult))
                op(TT(e1, e1, w1, ALU.mult))
                op(TT(oh1, oh1, wide(w1, 4), ALU.mult))
                op(TT(oh2, oh2, wide(e1, 4), ALU.mult))
                op(TT(oh1, oh1, oh2, ALU.add))
                TT(scratch[:, 0:2 * EXPERTS].rearrange("p (t g e) -> p t g e", t=NT, g=4),
                   first.unsqueeze(3).broadcast_to((P, NT, 4, 4)),
                   oh1.unsqueeze(2).broadcast_to((P, NT, 4, 4)), ALU.mult).then_inc(combine_ready, 1)
                dve.wait_ge(combine_turned, l + 1)
                nc.vector.tensor_copy(weightT[0:EXPERTS, :], acc[2][0:EXPERTS, 0:T]).then_inc(weightT_ready, 1)
                dve.wait_ge(spread_read, 2 * l + 2)
                gated_block(name, MOE_GROUPS, 1.0, GROUP0[name] - GROUP0["moe0"])

            def s_moba():
                norm("moba")
                norm_gain("moba", [("kv_norm_2", xnT), ("attn_norm_2", xqT)])
                rope("moba_k", 4, moba_k, "moba_cos", "moba_sin")
                for b in range(4):
                    wait_acc("moba_v", START["moba_v"] + 3, b)
                    nc.vector.tensor_copy(moba_v[:, b // 2, b % 2 * 512:b % 2 * 512 + 512], acc[b]).then_inc(acc_read, 1)
                rope("moba_q", 4, moba_q, "moba_cos", "moba_sin")
                attention(moba)
                add_to_x("moba_out", START["moba_out"] + 3, 1.0)

            def s_final():
                norm("final")
                dve.wait_ge(norm_scaled, NT * (NORM["final"] + 1))
                dve.wait_ge(gain_loaded, 32)
                nc.vector.tensor_tensor(final_out, xn, gain_row.unsqueeze(1).broadcast_to((P, NT, D)), ALU.mult)\
                    .then_inc(stored_ready, 1)

            s_ffn1()
            s_dil()
            s_rwkv_in()
            s_rwkv_solve()
            s_mix_out()
            s_ffn2()
            s_ret()
            s_moe(0)
            s_moba()
            s_moe(1)
            s_final()



_OUT = "out_0_dram"


def kernel(**inputs):
    import concourse.bacc as _bacc
    from concourse.bass_utils import run_bass_kernel_spmd as _run

    w = {k: np.asarray(v) for k, v in inputs.items()}
    nc = _bacc.Bacc("TRN2", target_bir_lowering=False, num_devices=1)
    arrays = {
        "in_stream": weight_stream(w), "in_params": param_table(w), "in_consts": const_table(),
        "in_x": np.ascontiguousarray(w["x"][0]), "in_gate_bias": np.ascontiguousarray(w["gate_bias"]),
        "in_gains": np.stack([w["final_norm"], w["final_norm_2"]]),
    }
    aps = [nc.dram_tensor(n, a.shape, F32, kind="ExternalInput").ap() for n, a in arrays.items()]
    aps.append(nc.dram_tensor(_OUT, (T, D), F32, kind="ExternalOutput").ap())
    two_blocks(nc, *aps)
    r = _run(nc, [arrays], core_ids=[0])
    return np.asarray(r.results[0][_OUT]).reshape(1, T, D)
```

```python
from contextlib import ExitStack
import math

import numpy as np
import concourse.bass as bass
from concourse import mybir

F32 = mybir.dt.float32
F32R = mybir.dt.float32r
ALU = mybir.AluOpType
ACT = mybir.ActivationFunctionType
AX = mybir.AxisListType

P = 128
T = 256
NT = T // P
D = 1024
KT = D // P
CH = 2048
CC = CH // KT
TW = CH // 2
RING = 3
AHEAD = 3
EPS = 1e-6

FFN_GROUPS = 2816 // CC
EXPERTS, D_EXPERT = 16, 512
MOE_GROUPS = EXPERTS * D_EXPERT // CC

DIL_HEADS, DIL_GROUPS, DIL_DH = 4, 3, 64
RW_HEADS, RW_N = 16, 64
PAIRS = RW_HEADS // 2
RET_HEADS, RET_DK, RET_DV = 4, 256, 512
MOBA_HEADS, MOBA_DH = 8, 128
AW = 3 * DIL_GROUPS * DIL_HEADS * DIL_DH
AQ = AW // 3
RS = 3 * D + 64 + 64 + 160
DECAY = math.exp(-0.5)
MASKED = -1e30



def swiglu_order(groups):
    order = [("gate", 0), ("up", 0)]
    for j in range(1, groups):
        order += [("gate", j), ("up", j), ("down", j - 1)]
    return order + [("down", groups - 1)]


PHASES = [
    ("ffn1", 3 * FFN_GROUPS),
    ("dil_qk", 2 * AQ // CC),
    ("dil_v", 4),
    ("lora", 1), ("lora_rest", 1), ("lora_g", 1),
    ("rkv", 3 * D // CC),
    ("gate_a", 4), ("gate_r", 4),
    ("attn_up", 1),
    ("rwkv_out", 4),
    ("mix_out", 4),
    ("ffn2", 3 * FFN_GROUPS),
    ("ret_qk", 2 * D // CC),
    ("ret_v", 8), ("ret_g", 8),
    ("ret_out", 8),
    ("moe0", 3 * MOE_GROUPS),
    ("moba_k", 4), ("moba_v", 4), ("moba_q", 4), ("moba_out", 4),
    ("moe1", 3 * MOE_GROUPS),
]
START = {}
NCHUNK = 0
for _name, _n in PHASES:
    START[_name] = NCHUNK
    NCHUNK += _n
NTILE = 2 * NCHUNK
assert NCHUNK % RING == 0 and 2 * RING % AHEAD == 0

ACC = {n: i for i, n in enumerate(
    ["ffn1", "dil_v", "gate_a", "gate_r", "attn_up", "rwkv_out", "mix_out", "ffn2", "ret_v0", "ret_v1",
     "ret_g0", "ret_g1", "ret_out", "moe0", "moba_v", "moba_out", "moe1"])}
NORM = {n: i for i, n in enumerate(["ffn1", "mix", "ffn2", "mid", "ret", "moe0", "moba", "moe1", "final"])}
TURN = {n: i for i, n in enumerate(["ffn1", "mix", "ffn2", "ret", "moe0", "moba", "moe1"])}
GROUP0 = {"ffn1": 0, "ffn2": FFN_GROUPS, "moe0": 2 * FFN_GROUPS, "moe1": 2 * FFN_GROUPS + MOE_GROUPS}
ROPE0 = {"dil": 0, "moba_k": 6, "moba_q": 10}
LORA_TILE = 8
ATT_TILE = 11


def columns_chunk(w, c0):
    return w[:, c0:c0 + CC].reshape(KT, P, 2, P).transpose(1, 2, 0, 3).reshape(P, CH)


def rows_chunk(w, r0):
    part = w[r0:r0 + 2 * P].reshape(2, P, w.shape[1]).transpose(1, 0, 2)
    return np.pad(part, ((0, 0), (0, 0), (0, D - w.shape[1]))).reshape(P, CH)


def weight_stream(w):
    out = []

    def put(a):
        out.append(np.pad(a, ((0, P - a.shape[0]), (0, CH - a.shape[1]))))

    def gated(gate, up, down, groups):
        for kind, j in swiglu_order(groups):
            if kind == "down":
                put(rows_chunk(down, j * CC))
            else:
                put(columns_chunk(gate if kind == "gate" else up, j * CC))

    def rows(m):
        for r in range(0, m.shape[0], 2 * P):
            put(rows_chunk(m, r))

    def cols(m):
        for c in range(0, m.shape[1], CC):
            put(columns_chunk(m, c))

    gated(w["ffn1_w_gate"][0], w["ffn1_w_up"][0], w["ffn1_w_down"][0], FFN_GROUPS)
    w_in = w["w_in"][0]
    cols(w_in[:, :2 * AQ])
    rows(w_in[:, 2 * AQ:AW])
    lora = w_in[:, AW + 3 * D:AW + RS]
    put(columns_chunk(lora, 0))
    rest = columns_chunk(np.pad(lora[:, CC:], ((0, 0), (0, CC - 32))), 0)[:, :TW]
    put(np.concatenate([rest, np.concatenate([w["rwkv_w2"][0], w["rwkv_a2"][0]], 0)], 1))
    g2 = w["rwkv_g2"][0]
    put(np.concatenate([g2[:P], np.pad(g2[P:], ((0, P - 32), (0, 0)))], 1))
    for c in (AW + D, AW, AW + 2 * D):
        cols(w_in[:, c:c + D])
    rows(w_in[:, AW + RS:AW + RS + D])
    rows(w_in[:, AW + RS + D:])
    rows(w["attn_w_up"][0])
    rows(w["rwkv_w_out"][0])
    rows(w["w_o"][0])
    gated(w["ffn2_w_gate"][0], w["ffn2_w_up"][0], w["ffn2_w_down"][0], FFN_GROUPS)
    ret = w["ret_w_in_2"][0]
    cols(ret[:, :2 * D])
    for c in range(2 * D, 6 * D, D):
        rows(ret[:, c:c + D])
    rows(w["ret_w_out_2"][0])

    def moe(layer):
        g, u, d = (w[f"expert_w_{n}_2"][layer].reshape(EXPERTS, *w[f"expert_w_{n}_2"].shape[3:])
                   for n in ("gate", "up", "down"))
        per = D_EXPERT // CC
        for kind, j in swiglu_order(MOE_GROUPS):
            e, c = j // per, j % per * CC
            put(rows_chunk(d[e], c) if kind == "down" else columns_chunk((g if kind == "gate" else u)[e], c))

    moe(0)
    cols(w["w_kv_2"][:, :D])
    rows(w["w_kv_2"][:, D:])
    cols(w["w_q_2"][0])
    rows(w["w_o_2"][0])
    moe(1)
    assert len(out) == NCHUNK
    return np.stack(out)



VECTORS = ["ffn1_norm", "mix_norm", "ffn2_norm", "ret_norm_2", "kv_norm_2", "attn_norm_2", "rwkv_w0",
           "rwkv_a0", "rwkv_k_k", "rwkv_k_a", "rwkv_r_k", "rwkv_ln_w", "rwkv_ln_b"]
PARAM = {}
_at = 0
for _name in VECTORS + ["ffn_norm_0", "ffn_norm_1"]:
    PARAM[_name] = _at
    _at += KT
PARAM["mu"] = _at
_at += 27
ROUTE = 20
for _l in range(2):
    PARAM[f"route_w{_l}"] = _at
    _at += KT * ROUTE
    PARAM[f"route_b{_l}"] = _at
    _at += ROUTE
NPARAM = _at


def param_table(w):
    def column(v):
        return np.asarray(v).reshape(KT, P).T

    parts = [column(w[n]) for n in VECTORS] + [column(w["ffn_norm_2"][l]) for l in range(2)]
    mu = w["rwkv_mu"][0]
    parts.append(mu[:3 * D].reshape(24, P).T)
    lora = np.pad(mu[3 * D:], (0, 3 * P - 288)).reshape(3, P).T
    parts.append(lora)
    for l in range(2):
        rw = np.concatenate([w["router_group_w_2"][l],
                             w["router_expert_w_2"][l].transpose(1, 0, 2).reshape(D, 16)], 1)
        parts.append(rw.reshape(KT, P, ROUTE).transpose(1, 0, 2).reshape(P, KT * ROUTE))
        rb = np.concatenate([w["router_group_b_2"][l], w["router_expert_b_2"][l].reshape(16)])
        parts.append(np.broadcast_to(rb, (P, ROUTE)))
    return np.concatenate(parts, 1)



CONST = {"ident": (0, P), "head_ones": (P, P)}
KEPT = 2 * P
_at = KEPT
for _name, _n in [("dil_swap", P), ("dil_cos", T), ("dil_sin", T), ("dil_mask0", 3 * P), ("dil_mask1", 3 * T),
                  ("tri_up", T), ("blk_up", P), ("blk_low", P), ("off_low", P), (None, 0),
                  ("moba_swap", P), ("ret_cos", T), ("ret_sin", T), ("moba_cos", T), ("moba_sin", T),
                  ("causal0", P), ("causal1", T), ("ret_decay", RET_HEADS * T)]:
    if _name is None:
        FIRST_END = _at
        continue
    CONST[_name] = (_at, _n)
    _at += _n
NCONST = _at
SECOND = NCONST - FIRST_END
TABLES = KEPT + max(SECOND, FIRST_END - KEPT)


def const_table():
    c = np.zeros((P, NCONST), np.float32)

    def put(name, a):
        at, n = CONST[name]
        c[:, at:at + n] = np.asarray(a, np.float64).reshape(P, n)

    i = np.arange(P)
    put("ident", np.eye(P))
    put("head_ones", (i[:, None] // 64 == i[None] // 64))
    pos = np.arange(T, dtype=np.float32)

    def rope(inv_freq, dh, half):
        ang = (pos[None, :] * inv_freq[:, None].astype(np.float32)).astype(np.float32)
        cos, sin, swap = np.ones((P, T)), np.zeros((P, T)), np.zeros((P, P))
        for a in range(P):
            d = a % dh
            if d < half:
                cos[a], sin[a], swap[a + half, a] = np.cos(ang[d]), -np.sin(ang[d]), 1
            elif d < 2 * half:
                cos[a], sin[a], swap[a - half, a] = np.cos(ang[d - half]), np.sin(ang[d - half]), 1
        return cos, sin, swap

    theta = np.float32(500000.0)
    cos, sin, swap = rope(np.power(theta, -np.arange(8, dtype=np.float32) * np.float32(2.0 / 16)), 64, 8)
    put("dil_cos", cos), put("dil_sin", sin), put("dil_swap", swap)
    cos, sin, swap = rope(np.float32(1) / theta ** (np.arange(16, dtype=np.float32) / np.float32(16)), 128, 16)
    put("moba_cos", cos), put("moba_sin", sin), put("moba_swap", swap)
    inv = np.float32(1) / np.float32(10000.0) ** (np.arange(128, dtype=np.float32) / np.float32(128))
    ang = (pos[None, :] * inv[:, None]).astype(np.float32)
    put("ret_cos", np.cos(ang)), put("ret_sin", np.sin(ang))
    for tile in range(NT):
        t = tile * P + i[:, None]
        s = np.arange(P * (tile + 1))[None]
        ok = [(t >= s) & ((t - s) % dil == 0) & (t - s <= win) for win, dil in ((128, 1), (512, 4), (2048, 16))]
        put(f"dil_mask{tile}", np.where(np.concatenate(ok, 1), 0.0, MASKED))
        put(f"causal{tile}", np.where(t >= s, 0.0, MASKED))
    up, same = i[:, None] < i[None], i[:, None] // 16 == i[None] // 16
    put("tri_up", np.concatenate([up, i[:, None] <= i[None]], 1))
    put("blk_up", up & same)
    put("blk_low", up.T & same)
    put("off_low", up.T & ~same)
    decay = []
    for h in range(RET_HEADS):
        gamma = np.log1p(-np.power(2.0, -5.0 - h))
        for off in (0, P):
            diff = i[None] + off - i[:, None]
            decay.append(np.where(diff >= 0, np.exp(gamma * np.maximum(diff, 0)), 0.0) * RET_DK ** -0.5)
    put("ret_decay", np.concatenate(decay, 1))
    return c


class Steps:

    def __init__(self, eng, sem):
        self.eng, self.sem, self.n = eng, sem, 0

    def did(self, ins):
        ins.then_inc(self.sem, 1)
        self.n += 1

    def settle(self):
        self.eng.wait_ge(self.sem, self.n)




def two_blocks(nc, stream, params, consts, x_in, gate_bias, gains, out):
    ctx = ExitStack()
    with ctx:
        def sb(name, *shape):
            return ctx.enter_context(nc.sbuf_tensor(name, [P, *shape], F32))

        def sem(name):
            return ctx.enter_context(nc.semaphore(name))

        def sbr(name, *shape):
            return ctx.enter_context(nc.sbuf_tensor(name, [P, *shape], F32R))

        ring = sb("ring", RING, CH)
        w_high, w_low = sbr("w_high", AHEAD, TW), sbr("w_low", AHEAD, TW)
        x_high, x_low = sbr("x_high", 2 * KT, T), sbr("x_low", 2 * KT, T)
        hid_high, hid_low = sbr("hid_high", 2, 2, T), sbr("hid_low", 2, 2, T)
        route_high, route_low = sbr("route_high", KT * ROUTE), sbr("route_low", KT * ROUTE)
        par = sb("par", NPARAM)
        con = sb("con", TABLES)
        x = sb("x", NT, D)
        small = sb("small", 224)
        ones = sb("ones", P)
        NA = 12
        arena = sb("arena", NA, CH)
        ps = ctx.enter_context(nc.psum_tensor("ps", [P, 8, 512], F32))
        wk = [ps[:, b, :] for b in range(4)]
        acc = [ps[:, 4 + b, :] for b in range(4)]
        accf = ps[:, 4:8, :].rearrange("p b n -> p (b n)")
        wkf = ps[:, 0:4, :].rearrange("p b n -> p (b n)")

        def A(i, n=1):
            return arena[:, i:i + n, :].rearrange("p a n -> p (a n)")

        def con_(name):
            at, n = CONST[name]
            at = at if at < FIRST_END else at - FIRST_END + KEPT
            return con[:, at:at + n]

        def par_(name, n=KT):
            return par[:, PARAM[name]:PARAM[name] + n]

        ident = con_("ident")
        xn = A(NA - 1).rearrange("p (t d) -> p t d", t=NT)
        junk = A(NA - 2).rearrange("p (t d) -> p t d", t=NT)
        ss, std, rstd = small[:, 0:2], small[:, 2:4], small[:, 4:6]
        sil = A(NA - 2)[:, 0:1024].rearrange("p (a f t) -> p a f t", a=2, f=2)
        hidT = A(NA - 2)[:, 1024:2048].rearrange("p (a f t) -> p a f t", a=2, f=2)

        def tiles(t, i, n=1):
            return t[:, i:i + n, :].rearrange("p k t -> p (k t)").bitcast(F32)

        landed = [sem(f"chunk_landed{s}") for s in range(RING)]
        w_high_ready, w_low_ready, tiles_used = sem("w_high_ready"), sem("w_low_ready"), sem("tiles_used")
        x_high_ready, x_low_ready = sem("x_high_ready"), sem("x_low_ready")
        hidden_whole, hidden_high, router_high, router_low = (sem(n) for n in (
            "hidden_whole", "hidden_high", "router_high", "router_low"))
        first_tables, second_tables = sem("first_tables"), sem("second_tables")
        x_loaded, tables_loaded, gain_loaded, bias_loaded = (sem(n) for n in (
            "x_loaded", "tables_loaded", "gain_loaded", "bias_loaded"))
        acc_done, acc_read = sem("acc_done"), sem("acc_read")
        norm_sum, norm_std, norm_scaled, norm_turned = (sem(n) for n in (
            "norm_sum", "norm_std", "norm_scaled", "norm_turned"))
        silu_done, hidden_ready, gated = sem("silu_done"), sem("hidden_ready"), sem("gated")
        rope_raw, rope_swapped, rope_used, rope_done = (sem(n) for n in (
            "rope_raw", "rope_swapped", "rope_used", "rope_done"))
        scores_ready, scores_read, bias_ready, exp_done, probs_ready, probs_turned, probsT_ready, heads_ready, \
            heads_read = (sem(n) for n in (
                "scores_ready", "scores_read", "bias_ready", "exp_done", "probs_ready", "probs_turned",
                "probsT_ready", "heads_ready", "heads_read"))
        dve_steps, act_steps = sem("dve_steps"), sem("act_steps")
        zeroed = sem("zeroed")
        lora_low, z_high, z_low, merge_high, merge_low, ret_high, ret_low = (sem(n) for n in (
            "lora_low", "z_high", "z_low", "merge_high", "merge_low", "ret_high", "ret_low"))
        z_copied, z_shifted = sem("z_copied"), sem("z_shifted")
        lora_act, lora_done, lora_by_act, lora_by_dve = (sem(n) for n in (
            "lora_act", "lora_done", "lora_by_act", "lora_by_dve"))
        kk_scaled, kk_squared, kk_summed, kk_root, kk_done = (sem(n) for n in (
            "kk_scaled", "kk_squared", "kk_summed", "kk_root", "kk_done"))
        cum_done, decays_done, rk_done, rk_summed, bonus_done, bk_decayed, tilde_done, turned_vbk, v_tok, bk_tok = (sem(n) for n in (
            "cum_done", "decays_done", "rk_done", "rk_summed", "bonus_done", "bk_decayed", "tilde_done", "turned_vbk", "v_tok",
            "bk_tok"))
        lane_pe = [sem(f"lane_pe{i}") for i in range(4)]
        lane_dve = [sem(f"lane_dve{i}") for i in range(4)]
        lane_act = [sem(f"lane_act{i}") for i in range(4)]
        y_centred, y_squared, y_var, y_std, y_normed, y_turned, y_affine, z_done = (sem(n) for n in (
            "y_centred", "y_squared", "y_var", "y_std", "y_normed", "y_turned", "y_affine", "z_done"))
        x_scaled, rot_read, rot_done, rs_ready, rs_masked, o_ready, o_summed, o_std, ret_y_done, ret_turned \
            = (sem(n) for n in (
                "x_scaled", "rot_read", "rot_done", "rs_ready", "rs_masked", "o_ready", "o_summed", "o_std",
                "ret_y_done", "ret_turned"))
        routed, route_shifted, route_exp, route_diff, route_exp2, combine_ready, combine_turned, weightT_ready, \
            spread, spread_read = (sem(n) for n in (
                "routed", "route_shifted", "route_exp", "route_diff", "route_exp2", "combine_ready",
                "combine_turned", "weightT_ready", "spread", "spread_read"))
        gate_done, merge_done, merge_turned = (sem(n) for n in (
            "gate_done", "merge_done", "merge_turned"))
        stored_ready, stored = sem("stored_ready"), sem("stored")

        block = ctx.enter_context(nc.Block())

        shifted = A(9)[:, 1028:1028 + 2 * T].rearrange("p (f t) -> p f t", f=2)

        def lane_counts(g, st):
            dve = min(g, 4) * 9 + max(g - 4, 0) * 8 + sum(n <= st for n in (1, 3, 4, 5, 6, 7, 8, 9))
            dve += (st >= 10 and g < 4)
            return dve, 7 * g + sum(n <= st for n in (2, 3, 4, 6, 7, 8, 10))

        class Att:
            def __init__(self, base, heads, groups, dh, scale, mask, q, k, v, outT):
                self.units = [(h, i) for h in range(heads) for i in range(NT)]
                self.base, self.groups, self.dh, self.scale = base, groups, dh, scale
                self.mask, self.q, self.k, self.v, self.outT = mask, q, k, v, outT

            def width(self, i):
                return self.groups * P * (i + 1)

        dil_qk = A(0, 2)[:, 0:12 * T].rearrange("p (k t) -> p k t", k=12)
        dil_v = A(2)[:, 0:2 * AQ].rearrange("p (t n) -> p t n", t=NT)
        moba_k = A(0).rearrange("p (k t) -> p k t", k=KT)
        moba_v = A(1).rearrange("p (t n) -> p t n", t=NT)
        moba_q = A(2).rearrange("p (k t) -> p k t", k=KT)
        prob = A(5, 2).rearrange("p (a n) -> p a n", a=4)
        probT = A(7).rearrange("p (a n) -> p a n", a=2)
        row_bias, row_sum, row_max, row_rsum = (lambda u, at=at: small[:, at + u % 4:at + u % 4 + 1]
                                                for at in (150, 154, 158, 162))
        raw = A(8)[:, 0:1024].rearrange("p (a n) -> p a n", a=2)
        turned = A(8)[:, 1024:2048].rearrange("p (a n) -> p a n", a=2)
        dil = Att(0, DIL_HEADS, 3, DIL_DH, DIL_DH ** -0.5, ("dil_mask0", "dil_mask1"),
                  lambda h, g: (dil_qk[64 * (h % 2):64 * (h % 2) + 64, 2 * g + h // 2, :]),
                  lambda h, g: (dil_qk[64 * (h % 2):64 * (h % 2) + 64, 6 + 2 * g + h // 2, :]),
                  lambda h, g, s: dil_v[:, s, (4 * g + h) * 64:(4 * g + h) * 64 + 64],
                  lambda t, h, i: t[64 * (h % 2):64 * (h % 2) + 64, ATT_TILE + h // 2, i * P:i * P + P])
        moba = Att(8, MOBA_HEADS, 1, MOBA_DH, MOBA_DH ** -0.5, ("causal0", "causal1"),
                   lambda h, g: moba_q[:, h, :], lambda h, g: moba_k[:, h, :],
                   lambda h, g, s: moba_v[:, s, h * P:h * P + P],
                   lambda t, h, i: t[:, h, i * P:i * P + P])

        def pairs(i):
            return A(i).rearrange("p (k t) -> p k t", k=PAIRS)

        def by_chunk(i):
            return A(i).rearrange("p (a t) -> p a t", t=P)

        R8, K8, V8, KK8, A8, C8, G8, BON = (pairs(i) for i in (0, 1, 2, 3, 4, 5, 10, 11))
        B8, KD8 = A8, K8
        AR = A(8, 2).rearrange("p (a s t) -> p a s t", s=2, t=P)
        zraw = A(9)[:, 0:4 * (T + 1)].rearrange("p (a f t) -> p a f t", a=2, f=2)
        zlora = A(8)[:, 0:3 * T].rearrange("p (f t) -> p f t", f=3)
        Vtok = A(5).rearrange("p (c n) -> p c n", c=2)
        BKtok = A(7).rearrange("p (c n) -> p c n", c=2)
        Ytok = A(6).rearrange("p (c n) -> p c n", c=2)
        LANE = 1280
        state = A(0)[:, 0:PAIRS * RW_N].rearrange("p (k n) -> p k n", k=PAIRS)
        lane = [A(0)[:, 640:640 + LANE], A(2, 2)[:, 0:LANE], A(2, 2)[:, LANE:2 * LANE], A(2, 2)[:, 2 * LANE:3 * LANE]]
        mbk = [l[:, 0:512] for l in lane]
        XD = [l[:, 512:896].rearrange("p (a n) -> p a n", a=3) for l in lane]
        NN = [l[:, 896:1152] for l in lane]
        NN2 = [l[:, 512:768] for l in lane]
        N4T = [l[:, 768:896] for l in lane]
        Wl = [l[:, 1152:1216] for l in lane]
        Ul = [l[:, 1216:1280] for l in lane]
        LO = [A(0)[:, 512:640], A(0)[:, 1920:2048], A(2, 2)[:, 3840:3968], A(2, 2)[:, 3968:4096]]
        mid, endf, startf = small[:, 24:40], small[:, 40:48], small[:, 48:64]
        gsum, gvar = small[:, 64:96], small[:, 96:128]
        zT = pairs(1)
        gate_a, gate_r, gbias, merged, mpart = (A(i) for i in (8, 9, 4, 5, 0))
        head_ones = con_("head_ones")

        ret_q, ret_k = pairs(0), pairs(1)
        ret_v, ret_g, ret_y = (A(i, 2).rearrange("p (t n) -> p t n", t=NT) for i in (2, 4, 6))
        ret_sT = A(8)[:, 0:4 * 384].rearrange("p (h n) -> p h n", h=RET_HEADS)
        ret_tmp = A(9).rearrange("p (a f t) -> p a f t", a=4, f=2)
        ret_ss, ret_std = small[:, 130:138], small[:, 138:146]
        by_expert = A(8, 2).rearrange("p (e t) -> p e t", e=EXPERTS)
        scratch = A(7)
        weightT = A(7)[:, 1024:1024 + T]
        gain_row = A(0)[:, 0:D]
        final_out = A(1).rearrange("p (t d) -> p t d", t=NT)

        @block.sync
        def _(sp):
            for s in range(RING):
                sp.dma_start(ring[:, s, :], stream[s]).then_inc(landed[s], 16)
            with sp.Fori(1, NCHUNK // RING) as i:
                for s in range(RING):
                    sp.wait_ge(w_low_ready, i * (2 * RING) + (2 * (s + 1) - 2 * RING))
                    sp.dma_start(ring[:, s, :], stream[bass.ds(i * RING + s, 1), :, :].rearrange("a p n -> p (a n)"))\
                        .then_inc(landed[s], 16)

        @block.gpsimd
        def _(pool):
            def low(t, turn=None):
                n = t + 1 - AHEAD
                pool.wait_ge(w_high_ready, t + 1 if turn is None else turn * (2 * RING) + (t + 1))
                if n > 0 or turn is not None:
                    pool.wait_ge(tiles_used, n if turn is None else turn * (2 * RING) + n)
                nc.gpsimd.tensor_tensor(w_low[:, t % AHEAD, :], ring[:, t // 2 % RING, t % 2 * TW:t % 2 * TW + TW],
                                        w_high[:, t % AHEAD, :].bitcast(F32), ALU.subtract).then_inc(w_low_ready, 1)

            for t in range(2 * RING):
                low(t)
            with pool.Fori(1, NCHUNK // RING) as i:
                for t in range(2 * RING):
                    low(t, i)

        @block.tensor
        def _(pe):
            def wait_tile(t, turn=None):
                pe.wait_ge(w_low_ready, t + 1 if turn is None else turn * 12 + (t + 1))

            def project(t, dst, x0=0, turn=None, signal=True, rows=slice(0, P), k_tiles=KT, at=0, arriving=None):
                wait_tile(t, turn)
                for k in range(k_tiles):
                    if arriving is not None and k % 2 == 0:
                        pe.wait_ge(x_low_ready, arriving + k + 2)
                    w = slice(at + k * P, at + k * P + P)
                    for n, (wp, xp) in enumerate(((w_high, x_high), (w_high, x_low), (w_low, x_high))):
                        mm = pe.matmul(dst, wp[rows, t % AHEAD, w], xp[rows, x0 + k, :],
                                       start=(k == 0 and n == 0), stop=(k == k_tiles - 1 and n == 2))
                if signal:
                    mm.then_inc(tiles_used, 1)
                return mm

            def project2(c, bank, x0=0, turn=None, arriving=None):
                project(2 * c, bank[:, 0:T], x0, turn, arriving=arriving)
                project(2 * c + 1, bank[:, T:2 * T], x0, turn)

            def add_rows(t, high, low, first, last, use, width=D, turn=None):
                wait_tile(t, turn)
                for tok in range(NT):
                    ts = slice(tok * P, tok * P + P)
                    for n, (xp, wp) in enumerate(((high, w_high), (high, w_low), (low, w_high))):
                        for half in range(2):
                            b = 2 * tok + half
                            n0, n1 = half * 512, min(half * 512 + 512, width)
                            if first and n == 0 and use:
                                pe.wait_ge(acc_read, 4 * (use - 1) + b + 1)
                            mm = pe.matmul(acc[b][:, 0:n1 - n0], xp[:, ts], wp[:, t % AHEAD, n0:n1],
                                           start=(first and n == 0), stop=(last and n == 2))
                            if last and n == 2 and b < 3:
                                mm.then_inc(acc_done, 1)
                mm.then_inc(tiles_used, 1)

            def accumulate(name, c, n, x0=0, width=D, pairs_ready=None):
                for j in range(2 * n):
                    if pairs_ready and j % 2 == 0:
                        pe.wait_ge(pairs_ready, j // 2 + 1)
                    add_rows(2 * c + j, x_high[:, x0 + j, :], x_low[:, x0 + j, :], j == 0, j == 2 * n - 1,
                             ACC[name], width)

            def norm(name):
                n = NORM[name]
                for tok in range(NT):
                    pe.wait_ge(norm_scaled, NT * n + tok + 1)
                    for k in range(KT):
                        at = k % 2 * T + tok * P
                        mm = pe.transpose(wk[k // 2][:, at:at + P], xn[:, tok, k * P:k * P + P], ident)
                        if tok == 1:
                            mm.then_inc(norm_turned, 1)

            def before_x(name):
                return KT * TURN[name] + (KT if TURN[name] > TURN["moba"] else 0)

            def gated_block(name, groups, before_down=None):
                c0, g0 = START[name], GROUP0[name]

                def gate_up(c, q, turn=None, arriving=None):
                    project2(c, wk[q], 0, turn, arriving)
                    project2(c + 1, wk[2 + q], 0, turn)

                def down(c, q, g, first=False, last=False, turn=None):
                    pe.wait_ge(hidden_ready, g0 + g + 1 if turn is None else turn * 2 + (g0 + g + 1))
                    for f in range(2):
                        add_rows(2 * c + f, hid_high[:, q, f, :], hid_low[:, q, f, :], first and f == 0,
                                 last and f == 1, ACC[name], D, turn)

                gate_up(c0, 0, arriving=before_x(name))
                gate_up(c0 + 2, 1)
                if before_down:
                    before_down()
                down(c0 + 4, 0, 0, first=True)
                with pe.Fori(0, (groups - 2) // 2) as i:
                    for q in range(2):
                        gate_up(c0 + 5 + 3 * q, q, i)
                        down(c0 + 7 + 3 * q, 1 - q, 1 + q, turn=i)
                for j in range((groups - 2) // 2 * 2 + 2, groups):
                    c = c0 + 2 + 3 * (j - 1)
                    gate_up(c, j % 2)
                    down(c + 2, (j - 1) % 2, j - 1)
                down(c0 + 3 * groups - 1, (groups - 1) % 2, groups - 1, last=True)

            def rope(name, c0, n, x0, swap, arriving=None):
                base = ROPE0[name]

                def swapped(m):
                    pe.wait_ge(rope_raw, base + m + 1)
                    if base + m >= 2:
                        pe.wait_ge(rope_used, base + m - 1)
                    pe.matmul(wk[2 + m % 2], con_(swap), raw[:, m % 2, :], start=True, stop=True)\
                        .then_inc(rope_swapped, 1)

                for m in range(n):
                    project2(c0 + m, wk[m % 2], x0, arriving=arriving if m == 0 else None)
                    if m:
                        swapped(m - 1)
                swapped(n - 1)

            def attention(a):
                def scores(u):
                    h, i = a.units[u]
                    if u >= 2:
                        pe.wait_ge(scores_read, a.base + u - 1)
                    w = P * (i + 1)
                    for g in range(a.groups):
                        at = 1024 * (u % 2) + g * w
                        mm = pe.matmul(wkf[:, at:at + w], a.q(h, g)[:, i * P:i * P + P], a.k(h, g)[:, 0:w],
                                       start=True, stop=True)
                    mm.then_inc(scores_ready, 1)

                def turn(u):
                    h, i = a.units[u]
                    pe.wait_ge(probs_ready, a.base + u + 1)
                    if u:
                        pe.wait_ge(probsT_ready, a.base + u)
                    for b in range(a.width(i) // P):
                        mm = pe.transpose(accf[:, b * P:b * P + P], prob[:, u % 4, b * P:b * P + P], ident)
                    mm.then_inc(probs_turned, 1)

                def heads(u):
                    h, i = a.units[u]
                    n = a.width(i) // P
                    pe.wait_ge(probsT_ready, a.base + u + 1)
                    if u >= 2:
                        pe.wait_ge(heads_read, a.base + u - 1)
                    row = 64 * (h % 2) if a.dh == 64 else 0
                    for b in range(n):
                        g, s = b // (i + 1), b % (i + 1)
                        mm = pe.matmul(acc[2 + u % 2][row:row + a.dh, 0:P], a.v(h, g, s),
                                       probT[:, u % 2, b * P:b * P + P], start=(b == 0), stop=(b == n - 1))
                    mm.then_inc(heads_ready, 1)

                n_units = len(a.units)
                scores(0)
                scores(1)
                for u in range(n_units):
                    if u + 2 < n_units:
                        scores(u + 2)
                    turn(u)
                    if u:
                        heads(u - 1)
                heads(n_units - 1)
                pe.wait_ge(heads_read, a.base + len(a.units))

            def s_ffn1():
                pe.wait_ge(tables_loaded, 32)
                norm("ffn1")
                gated_block("ffn1", FFN_GROUPS)

            def s_dil():
                norm("mix")
                pe.wait_ge(first_tables, 16)
                rope("dil", START["dil_qk"], 6, 0, "dil_swap", before_x("mix"))
                accumulate("dil_v", START["dil_v"], 4, 0, AQ)
                pe.wait_ge(rope_done, 6)
                pe.wait_ge(acc_read, 4 * (ACC["dil_v"] + 1))
                attention(dil)

            def s_rwkv_in():
                c = START["lora"]
                project2(c, wk[0])
                project(2 * c + 2, wk[1][:, 0:T])
                t_wa, t_g, t_g2 = 2 * c + 3, 2 * c + 4, 2 * c + 5
                pe.wait_ge(lora_low, 1)
                for r in range(4):
                    wb, ab, gb = (wk[2], wk[3], acc[0]) if r % 2 == 0 else (acc[1], acc[2], acc[3])
                    if r >= 2:
                        pe.wait_ge(lora_by_act, r - 1)
                        pe.wait_ge(lora_by_dve, r - 1)
                    for f in range(2):
                        project(t_wa, wb[:, f * T:f * T + T], LORA_TILE, None, False, slice(0, 64), 1, (2 * r + f) * P)
                    for f in range(2):
                        mm = project(t_wa, ab[:, f * T:f * T + T], LORA_TILE, None, False, slice(64, 128), 1,
                                     (2 * r + f) * P)
                    if r == 3:
                        mm.then_inc(tiles_used, 1)
                    wait_tile(t_g2)
                    for f in range(2):
                        w = slice((2 * r + f) * P, (2 * r + f) * P + P)
                        for rows, t, xt in ((slice(0, P), t_g, LORA_TILE + 1), (slice(0, 32), t_g2, LORA_TILE + 2)):
                            for n, (wp, xp) in enumerate(((w_high, x_high), (w_high, x_low), (w_low, x_high))):
                                mm = pe.matmul(gb[:, f * T:f * T + T], wp[rows, t % AHEAD, w], xp[rows, xt, :],
                                               start=(t == t_g and n == 0), stop=(t == t_g2 and n == 2))
                                if r == 3 and f == 1 and n == 2 and t == t_g:
                                    mm.then_inc(tiles_used, 1)
                    mm.then_inc(tiles_used if r == 3 else lora_done, 1)
                pe.wait_ge(lora_by_act, 3)
                pe.wait_ge(lora_by_dve, 3)
                for s in range(2, 14):
                    if s >= 4:
                        pe.wait_ge(z_copied, s - 3)
                    project2(START["rkv"] + s - 2, wk[s % 4])
                    if s == 7:
                        pe.wait_ge(lora_by_act, 4)
                        pe.wait_ge(lora_by_dve, 4)
                        pe.wait_ge(kk_squared, 1)
                        for b in range(4):
                            mm = pe.matmul(acc[b], head_ones, A(7)[:, b * 512:b * 512 + 512], start=True, stop=True)
                        mm.then_inc(kk_summed, 1)
                    if s == 12:
                        pe.wait_ge(kk_root, 1)
                        pe.wait_ge(rk_done, 1)
                        for b in range(4):
                            mm = pe.matmul(acc[b], head_ones, A(11)[:, b * 512:b * 512 + 512], start=True, stop=True)
                        mm.then_inc(rk_summed, 1)
                pe.wait_ge(z_copied, 14)
                pe.wait_ge(z_shifted, 14)
                for c in range(2):
                    for p in range(PAIRS):
                        mm = pe.transpose(wkf[:, c * D + p * P:c * D + p * P + P], V8[:, p, c * P:c * P + P], ident)
                mm.then_inc(turned_vbk, 1)
                pe.wait_ge(bonus_done, 1)
                pe.wait_ge(bk_decayed, 1)
                for n, src in enumerate((B8, KD8)):
                    for p in range(PAIRS):
                        mm = pe.transpose(accf[:, n * D + p * P:n * D + p * P + P], src[:, p, 0:P], ident)
                mm.then_inc(turned_vbk, 1)
                pe.wait_ge(v_tok, 1)
                pe.wait_ge(bk_tok, 1)
                pe.wait_ge(tilde_done, 1)

            def s_rwkv_solve():
                def unit(g, i):
                    h = 4 * (g % 4) + i
                    p, q, c = h // 2, h % 2, g // 4
                    return p, slice(64 * q, 64 * q + 64), c, slice(c * P, c * P + P), slice(64 * h, 64 * h + 64)

                def mm(out_, lhsT, rhs, start=True, stop=True):
                    return pe.matmul(out_, lhsT, rhs, start=start, stop=stop)

                for g in range(8):
                    for st in range(1, 11):
                        for i in range(4):
                            p, rows, c, ts, hc = unit(g, i)
                            a, b = wk[i], acc[i]
                            nd, na = lane_counts(g, st - 1)
                            if nd:
                                pe.wait_ge(lane_dve[i], nd)
                            if na:
                                pe.wait_ge(lane_act[i], na)
                            dT, tT, dd = (XD[i][:, n, :] for n in range(3))
                            n_, nT = NN[i][:, 0:P], NN[i][:, P:2 * P]
                            n2T, n2 = NN2[i][:, 0:P], NN2[i][:, P:2 * P]
                            if st == 1:
                                ar = AR[rows, 2 * p + c].rearrange("p s t -> p (s t)")
                                mm(a[:, 0:256], B8[rows, p, ts], ar)
                                mm(a[:, 256:512], KD8[rows, p, ts], ar)
                                last = mm(b[:, 0:P], AR[rows, 2 * p + c, 0, :], B8[rows, p, ts])
                            elif st == 2:
                                mm(a[:, 0:P], dd, dT)
                                mm(a[:, P:2 * P], dT, dd)
                                last = mm(a[:, 256:320], mbk[i][:, 256:384], Vtok[:, c, hc], stop=(c == 0))
                                if c:
                                    last = mm(a[:, 256:320], AR[rows, 2 * p + c, 0, :], state[rows, p, :], start=False)
                            elif st == 3:
                                mm(a[:, 0:P], dd, dT)
                                mm(a[:, P:2 * P], dT, dd)
                                last = mm(b[:, 0:P], dd, tT)
                            elif st == 4:
                                mm(a[:, 0:P], dT, dd)
                                last = mm(b[:, 0:P], dd, tT)
                            elif st == 5:
                                last = mm(b[:, 0:P], dd, tT)
                            elif st == 6:
                                mm(a[:, 0:P], tT, LO[i])
                                mm(a[:, P:2 * P], LO[i], tT)
                                last = mm(b[:, 0:64], tT, Wl[i])
                            elif st == 7:
                                mm(a[:, 0:P], n_, nT)
                                mm(a[:, P:2 * P], nT, n_)
                                last = mm(b[:, 0:64], nT, Ul[i])
                            elif st == 8:
                                mm(a[:, 0:P], n2, n2T)
                                last = mm(b[:, 0:64], n2T, Ul[i])
                            elif st == 9:
                                last = mm(b[:, 0:64], N4T[i], Ul[i])
                            else:
                                if c:
                                    mm(a[:, 0:64], AR[rows, 2 * p + c, 1, :], state[rows, p, :], stop=False)
                                mm(a[:, 0:64], mbk[i][:, 128:256], Ul[i], start=(c == 0), stop=False)
                                last = mm(a[:, 0:64], mbk[i][:, 384:512], Vtok[:, c, hc], start=False)
                                if c == 0:
                                    mm(b[rows, 0:64], BKtok[:, 0, hc], Ul[i], stop=False)
                                    last = mm(b[rows, 0:64], BKtok[:, 1, hc], Vtok[:, c, hc], start=False)
                            last.then_inc(lane_pe[i], 1)
                for i in range(4):
                    pe.wait_ge(lane_dve[i], lane_counts(7, 10)[0])
                    pe.wait_ge(lane_act[i], lane_counts(7, 10)[1])

            def s_mix_out():
                accumulate("gate_a", START["gate_a"], 4)
                pe.wait_ge(y_normed, 1)
                for p in range(PAIRS):
                    for c in range(2):
                        mm = pe.transpose(wk[p // 2][:, p % 2 * T + c * P:p % 2 * T + c * P + P],
                                          Ytok[:, c, p * P:p * P + P], ident)
                    if p % 2:
                        mm.then_inc(y_turned, 1)
                accumulate("gate_r", START["gate_r"], 4)
                accumulate("attn_up", START["attn_up"], 1, ATT_TILE)
                accumulate("rwkv_out", START["rwkv_out"], 4, pairs_ready=z_low)
                for tok in range(NT):
                    pe.wait_ge(merge_done, tok + 1)
                    for k in range(KT):
                        mm = pe.transpose(wk[k // 2][:, k % 2 * T + tok * P:k % 2 * T + tok * P + P],
                                          merged[:, tok * D + k * P:tok * D + k * P + P], ident)
                        if tok == 1 and k % 2:
                            mm.then_inc(merge_turned, 1)
                accumulate("mix_out", START["mix_out"], 4, pairs_ready=merge_low)

            def s_ffn2():
                norm("ffn2")
                gated_block("ffn2", FFN_GROUPS)

            def s_ret():
                norm("ret")
                for m in range(8):
                    if m >= 4:
                        pe.wait_ge(rot_read, m - 3)
                    project2(START["ret_qk"] + m, wk[m % 4], arriving=before_x("ret") if m == 0 else None)
                for n in range(2):
                    accumulate(f"ret_v{n}", START["ret_v"] + 4 * n, 4)
                pe.wait_ge(rot_done, 8)
                for h in range(RET_HEADS):
                    for s, t0, at in ((0, 0, 0), (1, P, T)):
                        for f in range(2):
                            mm = pe.matmul(wk[h][:, at:at + T - t0], ret_k[:, 2 * h + f, s * P:s * P + P],
                                           ret_q[:, 2 * h + f, t0:T], start=(f == 0), stop=(f == 1))
                    mm.then_inc(rs_ready, 1)
                for n in range(2):
                    accumulate(f"ret_g{n}", START["ret_g"] + 4 * n, 4)

                def outputs(h):
                    pe.wait_ge(rs_masked, h + 1)
                    for tok in range(NT):
                        bank = acc[2 * (h % 2) + tok]
                        if h >= 2:
                            pe.wait_ge(ret_y_done, NT * (h - 2) + tok + 1)
                        elif h == 0:
                            pe.wait_ge(acc_read, 4 * ACC["ret_g1"] + 4)
                        v = ret_v[:, :, h * RET_DV:(h + 1) * RET_DV]
                        mm = pe.matmul(bank, ret_sT[:, h, tok * P:tok * P + P], v[:, 0, :], start=True, stop=(tok == 0))
                        if tok:
                            mm = pe.matmul(bank, ret_sT[:, h, T:T + P], v[:, 1, :], start=False, stop=True)
                        mm.then_inc(o_ready, 1)

                def turn(h):
                    pe.wait_ge(ret_y_done, NT * h + NT)
                    if h >= 2:
                        pe.wait_ge(ret_low, h - 1)
                    for j in range(4):
                        for tok in range(NT):
                            at = 1024 * (h % 2) + j * T + tok * P
                            mm = pe.transpose(wkf[:, at:at + P], ret_y[:, tok, (4 * h + j) * P:(4 * h + j + 1) * P], ident)
                    mm.then_inc(ret_turned, 1)

                outputs(0)
                outputs(1)
                for h in range(RET_HEADS):
                    turn(h)
                    if h + 2 < RET_HEADS:
                        outputs(h + 2)
                pe.wait_ge(ret_low, RET_HEADS)
                accumulate("ret_out", START["ret_out"], 8)

            def s_moe(l):
                name = f"moe{l}"
                norm(name)
                pe.wait_ge(acc_read, 4 * ACC[name])
                pe.wait_ge(router_low, l + 1)
                for tok in range(NT):
                    for k in range(KT):
                        if tok == 0 and k % 2 == 0:
                            pe.wait_ge(x_low_ready, before_x(name) + k + 2)
                        for n, (xp, rp) in enumerate(((x_high, route_high), (x_high, route_low), (x_low, route_high))):
                            mm = pe.matmul(acc[tok][:, 0:ROUTE], xp[:, k, tok * P:tok * P + P],
                                           rp[:, k * ROUTE:k * ROUTE + ROUTE],
                                           start=(k == 0 and n == 0), stop=(k == KT - 1 and n == 2))
                mm.then_inc(routed, 1)

                def spread_weights():
                    pe.wait_ge(combine_ready, l + 1)
                    for tok in range(NT):
                        mm = pe.transpose(acc[2][0:EXPERTS, tok * P:tok * P + P],
                                          scratch[:, tok * EXPERTS:tok * EXPERTS + EXPERTS], ident)
                    mm.then_inc(combine_turned, 1)
                    pe.wait_ge(weightT_ready, l + 1)
                    for part in range(4):
                        if part >= 2:
                            pe.wait_ge(spread_read, 4 * l + part - 1)
                        for e in range(4):
                            n, at = 4 * part + e, 1024 * (part % 2) + e * T
                            mm = pe.matmul(accf[:, at:at + T], ident[0:EXPERTS, n:n + 1].broadcast_to((EXPERTS, P)),
                                           weightT[0:EXPERTS, :], start=True, stop=True)
                        mm.then_inc(spread, 1)
                    pe.wait_ge(spread_read, 4 * l + 4)

                gated_block(name, MOE_GROUPS, spread_weights)

            def s_moba():
                norm("moba")
                pe.wait_ge(x_low_ready, before_x("moba") + 2 * KT)
                rope("moba_k", START["moba_k"], 4, 0, "moba_swap")
                accumulate("moba_v", START["moba_v"], 4)
                rope("moba_q", START["moba_q"], 4, KT, "moba_swap")
                pe.wait_ge(rope_done, 14)
                pe.wait_ge(acc_read, 4 * (ACC["moba_v"] + 1))
                attention(moba)
                accumulate("moba_out", START["moba_out"], 4)

            def s_final():
                pass

            s_ffn1()
            s_dil()
            s_rwkv_in()
            s_rwkv_solve()
            s_mix_out()
            s_ffn2()
            s_ret()
            s_moe(0)
            s_moba()
            s_moe(1)
            s_final()

        @block.scalar
        def _(act):
            own = Steps(act, act_steps)
            act.dma_start(x[:, :, :], x_in.rearrange("(t p) d -> p t d", p=P)).then_inc(x_loaded, 16)
            act.dma_start(con[:, 0:KEPT], consts[:, 0:KEPT]).then_inc(tables_loaded, 16)
            act.dma_start(par[:, :], params).then_inc(tables_loaded, 16)
            act.dma_start(con[:, KEPT:FIRST_END], consts[:, KEPT:FIRST_END]).then_inc(first_tables, 16)
            split_next = [0]

            def split(t, turn=None):
                c, n = t // 2, t + 1 - AHEAD
                v = 16 * (c // RING + 1)
                if t % 2 == 0:
                    act.wait_ge(landed[c % RING], v if turn is None else turn * 32 + v)
                if n > 0:
                    act.wait_ge(tiles_used, n if turn is None else turn * 12 + n)
                nc.scalar.activation(w_high[:, t % AHEAD, :], ring[:, c % RING, t % 2 * TW:t % 2 * TW + TW], ACT.Copy)\
                    .then_inc(w_high_ready, 1)

            def split_to(end):
                while split_next[0] < min(end, NTILE):
                    split(split_next[0])
                    split_next[0] += 1

            def used(n):
                split_to(n + AHEAD - 1)
                act.wait_ge(tiles_used, n)

            def norm(name, prev):
                n = NORM[name]
                act.wait_ge(zeroed, 1)
                nc.scalar.activation(small[:, 10:11], small[:, 8:9], ACT.Sqrt)
                if prev is None:
                    act.wait_ge(x_loaded, 16)
                elif prev == "mid":
                    act.wait_ge(x_scaled, 1)
                for tok in range(NT):
                    if prev not in (None, "mid"):
                        act.wait_ge(acc_read, 4 * ACC[prev] + 2 * tok + 2)
                    nc.scalar.activation(junk[:, tok, :], x[:, tok, :], ACT.Square, accum_out=ss[:, tok:tok + 1])\
                        .then_inc(norm_sum, 1)
                act.wait_ge(norm_sum, NT * (n + 1))
                nc.scalar.activation(std, ss, ACT.Sqrt, bias=small[:, 8:9], scale=1.0 / D).then_inc(norm_std, 1)

            def norm_gain(name, outs):
                n = TURN[name]
                base = 8 * n + (8 if n > TURN["moba"] else 0)
                for m, (gain, x0) in enumerate(outs):
                    for k in range(KT):
                        act.wait_ge(norm_turned, KT * n + (k | 1) + 1)
                        if m:
                            act.wait_ge(x_low_ready, base + (k | 1) + 1)
                        nc.scalar.activation(x_high[:, x0 + k, :], wk[k // 2][:, k % 2 * T:k % 2 * T + T], ACT.Copy,
                                             scale=par_(gain)[:, k:k + 1]).then_inc(x_high_ready, 1)

            def gated_block(name, groups, after_two=None):
                t0 = 2 * START[name]

                def silu(n, q, turn=None):
                    act.wait_ge(tiles_used, n if turn is None else turn * 12 + n)
                    nc.scalar.activation(sil[:, q].rearrange("p f t -> p (f t)"), wk[q], ACT.Silu)\
                        .then_inc(silu_done, 1)

                split_to(t0 + 2 + AHEAD - 1)
                silu(t0 + 2, 0)
                split_to(t0 + 6 + AHEAD - 1)
                silu(t0 + 6, 1)
                if after_two:
                    split_to(t0 + 8 + AHEAD)
                    after_two()
                    split_next[0] = t0 + 8 + AHEAD
                split_to(t0 + 8 + AHEAD)
                loops = (groups - 2) // 2
                with act.Fori(0, loops) as i:
                    for q in range(2):
                        for t in range(6):
                            split(t0 + 8 + AHEAD + 6 * q + t, i)
                            if t == 3:
                                silu(t0 + 12 + 6 * q, q, i)
                split_next[0] += 12 * loops
                for j in range(2 * loops + 2, groups):
                    split_to(t0 + 6 * j + AHEAD - 1)
                    silu(t0 + 6 * j, j % 2)

            def rope(name, c0, n):
                base = ROPE0[name]
                for m in range(n):
                    used(2 * (c0 + m + 1))
                    if base + m >= 2:
                        act.wait_ge(rope_used, base + m - 1)
                    nc.scalar.activation(raw[:, m % 2, :], wk[m % 2], ACT.Copy).then_inc(rope_raw, 1)

            def attention(a):
                def exps(u):
                    h, i = a.units[u]
                    act.wait_ge(bias_ready, a.base + u + 1)
                    s = prob[:, u % 4, 0:a.width(i)]
                    nc.scalar.activation(s, s, ACT.Exp, bias=row_bias(u), scale=a.scale, accum_out=row_sum(u))\
                        .then_inc(exp_done, 1)

                def evacuate(u):
                    h, i = a.units[u]
                    act.wait_ge(probs_turned, a.base + u + 1)
                    if u >= 2:
                        act.wait_ge(heads_ready, a.base + u - 1)
                    nc.scalar.activation(probT[:, u % 2, 0:a.width(i)], accf[:, 0:a.width(i)], ACT.Copy)\
                        .then_inc(probsT_ready, 1)

                exps(0)
                for u in range(len(a.units)):
                    if u + 1 < len(a.units):
                        exps(u + 1)
                    evacuate(u)

            def s_ffn1():
                norm("ffn1", None)
                split_to(AHEAD)
                act.wait_ge(tables_loaded, 32)
                norm_gain("ffn1", [("ffn1_norm", 0)])
                gated_block("ffn1", FFN_GROUPS)
                used(2 * START["dil_qk"])

            def s_dil():
                norm("mix", "ffn1")
                norm_gain("mix", [("mix_norm", 0)])
                rope("dil", START["dil_qk"], 6)
                used(2 * START["lora"])
                attention(dil)

            def s_rwkv_in():
                def raw_z(s, bank, rows=P, f=2):
                    if s >= 2:
                        act.wait_ge(z_shifted, s - 1)
                    nc.scalar.activation(zraw[0:rows, s % 2, 0:f, 1:T + 1],
                                         bank[0:rows, 0:f * T].rearrange("p (f t) -> p f t", f=f), ACT.Copy)\
                        .then_inc(z_copied, 1)

                act.wait_ge(zeroed, 2)
                used(2 * START["lora"] + 2)
                raw_z(0, wk[0])
                used(2 * START["lora"] + 3)
                raw_z(1, wk[1], 32, 1)
                split_to(2 * START["rkv"])
                act.wait_ge(z_shifted, 2)
                nc.scalar.activation(zlora[0:64, 0, :], zlora[0:64, 0, :], ACT.Tanh).then_inc(lora_act, 1)
                nc.scalar.activation(zlora[:, 1, :], zlora[:, 1, :], ACT.Sigmoid).then_inc(lora_act, 1)
                nc.scalar.activation(zlora[0:32, 2, :], zlora[0:32, 2, :], ACT.Sigmoid).then_inc(lora_act, 1)
                for r in range(4):
                    wb, ab = (wk[2], wk[3]) if r % 2 == 0 else (acc[1], acc[2])
                    if r < 3:
                        act.wait_ge(lora_done, r + 1)
                    else:
                        act.wait_ge(tiles_used, 2 * START["rkv"])
                    for f in range(2):
                        p = 2 * r + f
                        nc.scalar.activation(C8[:, p, :], wb[:, f * T:f * T + T], ACT.Sigmoid,
                                             bias=par_("rwkv_w0")[:, p:p + 1])
                        ins = nc.scalar.activation(A8[:, p, :], ab[:, f * T:f * T + T], ACT.Sigmoid,
                                                   bias=par_("rwkv_a0")[:, p:p + 1])
                    ins.then_inc(lora_by_act, 1)
                for s in range(2, 14):
                    used(2 * (START["rkv"] + s - 1))
                    raw_z(s, wk[s % 4])
                    if s == 6:
                        act.wait_ge(kk_scaled, 1)
                        nc.scalar.activation(A(7), A(3), ACT.Square).then_inc(kk_squared, 1)
                    if s == 8:
                        act.wait_ge(kk_summed, 1)
                        nc.scalar.activation(A(6), accf, ACT.Sqrt).then_inc(kk_root, 1)
                    if s == 11:
                        act.wait_ge(cum_done, 1)
                        act.wait_ge(kk_done, 1)
                        nc.scalar.activation(endf, endf, ACT.Exp, scale=-DECAY)
                        nc.scalar.activation(startf, startf, ACT.Exp, scale=DECAY)
                        nc.scalar.activation(A(6), A(5), ACT.Exp, scale=-DECAY)
                        nc.scalar.activation(A(7), A(5), ACT.Exp, scale=DECAY).then_inc(decays_done, 1)
                act.wait_ge(turned_vbk, 1)
                act.wait_ge(decays_done, 1)
                nc.scalar.activation(A(5), wkf, ACT.Copy).then_inc(v_tok, 1)
                act.wait_ge(turned_vbk, 2)
                nc.scalar.activation(A(7), accf, ACT.Copy).then_inc(bk_tok, 1)

            def s_rwkv_solve():
                for g in range(8):
                    for st in range(2, 11):
                        if st in (5, 9):
                            continue
                        for i in range(4):
                            h, c = 4 * (g % 4) + i, g // 4
                            act.wait_ge(lane_pe[i], 10 * g + st)
                            a = wk[i]
                            two = a[:, 0:256].rearrange("p (n t) -> p n t", n=2)
                            if st == 2:
                                nc.scalar.activation(XD[i][:, 0::2, :], two, ACT.Copy)
                                ins = nc.scalar.activation(Wl[i], a[:, 256:320], ACT.Copy)
                            elif st == 3:
                                ins = nc.scalar.activation(XD[i][:, 0::2, :], two, ACT.Copy)
                            elif st == 4:
                                ins = nc.scalar.activation(XD[i][:, 2, :], a[:, 0:P], ACT.Copy)
                            elif st == 6:
                                ins = nc.scalar.activation(NN[i], a[:, 0:256], ACT.Copy)
                            elif st == 7:
                                ins = nc.scalar.activation(NN2[i], a[:, 0:256], ACT.Copy)
                            elif st == 8:
                                ins = nc.scalar.activation(N4T[i], a[:, 0:P], ACT.Copy)
                            else:
                                ins = nc.scalar.activation(Ytok[:, c, 64 * h:64 * h + 64], a[:, 0:64], ACT.Copy)
                            ins.then_inc(lane_act[i], 1)

            def s_mix_out():
                for i in range(4):
                    act.wait_ge(lane_pe[i], 80)
                act.dma_start(gbias, gate_bias.broadcast_to((P, 2 * D))).then_inc(bias_loaded, 16)
                split_to(2 * START["gate_a"] + AHEAD)
                act.wait_ge(y_centred, 1)
                nc.scalar.activation(A(0), A(6), ACT.Square).then_inc(y_squared, 1)
                split_to(2 * START["gate_a"] + 2 + AHEAD)
                act.wait_ge(y_var, 1)
                nc.scalar.activation(gvar, gvar, ACT.Sqrt, bias=small[:, 9:10], scale=1.0 / RW_N).then_inc(y_std, 1)
                used(2 * START["gate_r"])
                split_to(2 * START["gate_r"] + AHEAD)
                for p in range(PAIRS):
                    act.wait_ge(y_turned, p // 2 + 1)
                    nc.scalar.activation(zT[:, p, :], wk[p // 2][:, p % 2 * T:p % 2 * T + T], ACT.Identity,
                                         bias=par_("rwkv_ln_b")[:, p:p + 1], scale=par_("rwkv_ln_w")[:, p:p + 1])\
                        .then_inc(y_affine, 1)
                split_to(2 * START["gate_r"] + 2 + AHEAD)
                act.wait_ge(acc_read, 4 * (ACC["gate_a"] + 1))
                nc.scalar.activation(gate_a, gate_a, ACT.Sigmoid).then_inc(gate_done, 1)
                used(2 * START["attn_up"])
                split_to(2 * START["attn_up"] + AHEAD)
                act.wait_ge(z_done, 1)
                for b in range(4):
                    nc.scalar.activation(x_high[:, 2 * b:2 * b + 2, :], zT[:, 2 * b:2 * b + 2, :], ACT.Copy)\
                        .then_inc(z_high, 1)
                act.wait_ge(acc_read, 4 * (ACC["gate_r"] + 1))
                nc.scalar.activation(gate_r, gate_r, ACT.Sigmoid).then_inc(gate_done, 1)
                used(2 * START["mix_out"])
                for b in range(4):
                    act.wait_ge(merge_turned, b + 1)
                    nc.scalar.activation(x_high[:, 2 * b:2 * b + 2, :], wk[b].rearrange("p (k t) -> p k t", t=T), ACT.Copy)\
                        .then_inc(merge_high, 1)
                used(2 * START["ffn2"])

            def s_ffn2():
                norm("ffn2", "mix_out")
                act.dma_start(gain_row, gains[0:1, :].broadcast_to((P, D))).then_inc(gain_loaded, 16)
                act.dma_start(con[:, KEPT:KEPT + SECOND], consts[:, FIRST_END:NCONST]).then_inc(second_tables, 16)
                norm_gain("ffn2", [("ffn2_norm", 0)])
                gated_block("ffn2", FFN_GROUPS)
                used(2 * START["ret_qk"])

            def s_ret():
                norm("mid", "ffn2")
                norm("ret", "mid")
                norm_gain("ret", [("ret_norm_2", 0)])
                for n in range(2):
                    split_to(2 * (START["ret_g"] + 4 * n + 4) + AHEAD - 1)
                    for b in range(4):
                        if b < 3:
                            act.wait_ge(acc_done, 3 * ACC[f"ret_g{n}"] + b + 1)
                        else:
                            act.wait_ge(tiles_used, 2 * (START["ret_g"] + 4 * n + 4))
                        at = n * D + b % 2 * 512
                        nc.scalar.activation(ret_g[:, b // 2, at:at + 512], acc[b], ACT.Silu).then_inc(acc_read, 1)

                def sums(h):
                    for tok in range(NT):
                        u = NT * h + tok
                        act.wait_ge(o_ready, u + 1)
                        nc.scalar.activation(A(10)[:, tok * 512:tok * 512 + 512], acc[2 * (h % 2) + tok], ACT.Square,
                                             accum_out=ret_ss[:, u:u + 1]).then_inc(o_summed, 1)
                    act.wait_ge(o_summed, NT * h + NT)
                    nc.scalar.activation(ret_std[:, NT * h:NT * h + NT], ret_ss[:, NT * h:NT * h + NT], ACT.Sqrt,
                                         bias=small[:, 8:9], scale=1.0 / RET_DV).then_inc(o_std, 1)

                def copy(h):
                    act.wait_ge(ret_turned, h + 1)
                    bank = wkf[:, 1024 * (h % 2):1024 * (h % 2) + 1024].rearrange("p (k t) -> p k t", t=T)
                    nc.scalar.activation(x_high[:, 4 * h:4 * h + 4, :], bank, ACT.Copy).then_inc(ret_high, 1)

                sums(0)
                sums(1)
                for h in range(RET_HEADS):
                    copy(h)
                    if h + 2 < RET_HEADS:
                        sums(h + 2)
                used(2 * START["moe0"])

            def s_moe(l):
                name = f"moe{l}"
                nc.scalar.activation(route_high[:, :], par_(f"route_w{l}", KT * ROUTE), ACT.Copy).then_inc(router_high, 1)
                norm(name, ("ret_out", "moba_out")[l])
                norm_gain(name, [(f"ffn_norm_{l}", 0)])
                split_to(2 * START[name] + 2 + AHEAD)
                act.wait_ge(route_shifted, l + 1)
                e4, e1 = scratch[:, 100:108], scratch[:, 150:152]
                nc.scalar.activation(e4, e4, ACT.Exp).then_inc(route_exp, 1)
                split_to(2 * START[name] + 4 + AHEAD)
                act.wait_ge(route_diff, l + 1)
                nc.scalar.activation(e1, e1, ACT.Exp).then_inc(route_exp2, 1)

                def spread_copies():
                    for part in range(4):
                        act.wait_ge(spread, 4 * l + part + 1)
                        at = 1024 * (part % 2)
                        nc.scalar.activation(A(8, 2)[:, 1024 * part:1024 * part + 1024], accf[:, at:at + 1024], ACT.Copy)\
                            .then_inc(spread_read, 1)

                gated_block(name, MOE_GROUPS, spread_copies)
                used(2 * (START[name] + 3 * MOE_GROUPS))

            def s_moba():
                norm("moba", "moe0")
                norm_gain("moba", [("kv_norm_2", 0), ("attn_norm_2", KT)])
                rope("moba_k", START["moba_k"], 4)
                rope("moba_q", START["moba_q"], 4)
                attention(moba)
                used(2 * START["moe1"])

            def s_final():
                act.dma_start(gain_row, gains[1:2, :].broadcast_to((P, D))).then_inc(gain_loaded, 16)
                norm("final", "moe1")
                act.wait_ge(stored_ready, 1)
                act.dma_start(out.rearrange("(t p) d -> p t d", p=P), final_out).then_inc(stored, 16)
                act.wait_ge(stored, 16)

            s_ffn1()
            s_dil()
            s_rwkv_in()
            s_rwkv_solve()
            s_mix_out()
            s_ffn2()
            s_ret()
            s_moe(0)
            s_moba()
            s_moe(1)
            s_final()

        @block.vector
        def _(dve):
            own = Steps(dve, dve_steps)
            nc.vector.memset(ones[:, :], 1.0)
            nc.vector.memset(small[:, 9:10], 64e-5)
            for n in range(4):
                nc.vector.memset(small[:, 12 + n:13 + n], 4.0 - n)
            nc.vector.memset(small[:, 8:9], EPS).then_inc(zeroed, 1)

            def norm(name):
                n = NORM[name]
                dve.wait_ge(norm_std, n + 1)
                own.did(nc.vector.reciprocal(rstd, std))
                own.settle()
                for tok in range(NT):
                    nc.vector.tensor_scalar(xn[:, tok, :], x[:, tok, :], rstd[:, tok:tok + 1], None, ALU.mult)\
                        .then_inc(norm_scaled, 1)

            def norm_gain(name, outs):
                n = TURN[name]
                base = 8 * n + (8 if n > TURN["moba"] else 0)
                for m, (gain, x0) in enumerate(outs):
                    for k in range(KT):
                        dve.wait_ge(x_high_ready, base + 8 * m + (k | 1) + 1)
                        nc.vector.scalar_tensor_tensor(
                            out=x_low[:, x0 + k, :], in0=wk[k // 2][:, k % 2 * T:k % 2 * T + T],
                            scalar=par_(gain)[:, k:k + 1], in1=tiles(x_high, x0 + k), op0=ALU.mult,
                            op1=ALU.subtract).then_inc(x_low_ready, 1)

            def wait_acc(name, last_chunk, b):
                if b < 3:
                    dve.wait_ge(acc_done, 3 * ACC[name] + b + 1)
                else:
                    dve.wait_ge(tiles_used, 2 * (last_chunk + 1))

            def add_to_x(name, last_chunk, scale):
                for b in range(4):
                    wait_acc(name, last_chunk, b)
                    part = x[:, b // 2, b % 2 * 512:b % 2 * 512 + 512]
                    nc.vector.scalar_tensor_tensor(out=part, in0=acc[b], scalar=scale, in1=part, op0=ALU.mult,
                                                   op1=ALU.add).then_inc(acc_read, 1)

            def gated_block(name, groups, scale, weight=None):
                c0, g0 = START[name], GROUP0[name]

                def hidden(c, q, g, turn=None):
                    n = g0 + g + 1
                    dve.wait_ge(tiles_used, 2 * (c + 1) if turn is None else turn * 12 + 2 * (c + 1))
                    dve.wait_ge(silu_done, n if turn is None else turn * 2 + n)
                    whole = hidT[:, q].rearrange("p f t -> p (f t)")
                    mul = nc.vector.tensor_tensor(whole, sil[:, q].rearrange("p f t -> p (f t)"), wk[2 + q], ALU.mult)
                    if weight is None:
                        mul.then_inc(hidden_whole, 1)
                    else:
                        mul.then_inc(gated, 1)
                        m = weight + g + 1
                        dve.wait_ge(gated, m if turn is None else turn * 2 + m)
                        we = by_expert[:, g // 2:g // 2 + 1, :] if turn is None else \
                            by_expert[:, bass.ds(turn + g // 2, 1), :]
                        nc.vector.tensor_tensor(hidT[:, q], hidT[:, q], we.broadcast_to((P, 2, T)), ALU.mult)\
                            .then_inc(hidden_whole, 1)
                    dve.wait_ge(hidden_whole, n if turn is None else turn * 2 + n)
                    high = hid_high[:, q].rearrange("p f t -> p (f t)")
                    nc.vector.tensor_copy(high, whole).then_inc(hidden_high, 1)
                    dve.wait_ge(hidden_high, n if turn is None else turn * 2 + n)
                    nc.vector.tensor_tensor(hid_low[:, q].rearrange("p f t -> p (f t)"), whole, high.bitcast(F32),
                                            ALU.subtract).then_inc(hidden_ready, 1)

                hidden(c0 + 1, 0, 0)
                hidden(c0 + 3, 1, 1)
                if weight is not None:
                    dve.wait_ge(spread_read, 4 * (weight // MOE_GROUPS) + 4)
                with dve.Fori(0, (groups - 2) // 2) as i:
                    for q in range(2):
                        hidden(c0 + 6 + 3 * q, q, 2 + q, i)
                for j in range((groups - 2) // 2 * 2 + 2, groups):
                    hidden(c0 + 3 + 3 * (j - 1), j % 2, j)
                add_to_x(name, c0 + 3 * groups - 1, scale)

            def rope(name, n, dst, cos, sin):
                base = ROPE0[name]
                cs, sn = (con_(t).unsqueeze(1).broadcast_to((P, 2, T)) for t in (cos, sin))
                for m in range(n):
                    dve.wait_ge(rope_raw, base + m + 1)
                    r = raw[:, m % 2, :].rearrange("p (f t) -> p f t", f=2)
                    d = dst[:, 2 * m:2 * m + 2, :]
                    tmp = turned[:, m % 2, :].rearrange("p (f t) -> p f t", f=2)
                    own.did(nc.vector.tensor_tensor(d, r, cs, ALU.mult))
                    dve.wait_ge(rope_swapped, base + m + 1)
                    nc.vector.tensor_tensor(tmp, wk[2 + m % 2].rearrange("p (f t) -> p f t", f=2), sn, ALU.mult)\
                        .then_inc(rope_used, 1)
                    own.settle()
                    dve.wait_ge(rope_used, base + m + 1)
                    nc.vector.tensor_tensor(d, d, tmp, ALU.add).then_inc(rope_done, 1)

            def attention(a):
                def masked(u):
                    h, i = a.units[u]
                    w = a.width(i)
                    dve.wait_ge(scores_ready, a.base + u + 1)
                    if u >= 4:
                        dve.wait_ge(probs_turned, a.base + u - 3)
                    s = prob[:, u % 4, 0:w]
                    nc.vector.tensor_tensor(s, wkf[:, 1024 * (u % 2):1024 * (u % 2) + w], con_(a.mask[i]), ALU.add)\
                        .then_inc(scores_read, 1)
                    dve.wait_ge(scores_read, a.base + u + 1)
                    own.did(nc.vector.tensor_reduce(row_max(u), s, AX.X, ALU.max))
                    own.settle()
                    nc.vector.tensor_scalar(row_bias(u), row_max(u), -a.scale, None, ALU.mult)\
                        .then_inc(bias_ready, 1)

                def normalised(u):
                    h, i = a.units[u]
                    dve.wait_ge(exp_done, a.base + u + 1)
                    own.did(nc.vector.reciprocal(row_rsum(u), row_sum(u)))
                    own.settle()
                    s = prob[:, u % 4, 0:a.width(i)]
                    nc.vector.tensor_scalar(s, s, row_rsum(u), None, ALU.mult).then_inc(probs_ready, 1)

                def evacuate(u):
                    h, i = a.units[u]
                    row = 64 * (h % 2) if a.dh == 64 else 0
                    dve.wait_ge(heads_ready, a.base + u + 1)
                    bank = acc[2 + u % 2][row:row + a.dh, 0:P]
                    own.did(nc.vector.tensor_copy(a.outT(x_high, h, i), bank))
                    own.settle()
                    nc.vector.tensor_tensor(a.outT(x_low, h, i), bank, a.outT(x_high, h, i).bitcast(F32), ALU.subtract)\
                        .then_inc(heads_read, 1)

                masked(0)
                masked(1)
                for u in range(len(a.units)):
                    normalised(u)
                    if u + 2 < len(a.units):
                        masked(u + 2)
                    if u:
                        evacuate(u - 1)
                evacuate(len(a.units) - 1)

            def s_ffn1():
                norm("ffn1")
                dve.wait_ge(tables_loaded, 32)
                norm_gain("ffn1", [("ffn1_norm", 0)])
                gated_block("ffn1", FFN_GROUPS, 0.5)

            def s_dil():
                norm("mix")
                norm_gain("mix", [("mix_norm", 0)])
                dve.wait_ge(first_tables, 16)
                rope("dil", 6, dil_qk, "dil_cos", "dil_sin")
                for b in range(4):
                    wait_acc("dil_v", START["dil_v"] + 3, b)
                    n0 = b % 2 * 512
                    n1 = min(n0 + 512, AQ)
                    nc.vector.tensor_copy(dil_v[:, b // 2, n0:n1], acc[b][:, 0:n1 - n0]).then_inc(acc_read, 1)
                attention(dil)

            def s_rwkv_in():
                nc.vector.memset(zraw[:, :, :, 0:1], 0.0).then_inc(zeroed, 1)
                dve.wait_ge(zeroed, 2)

                def shift(s, outs, mus, rows=P):
                    f = len(outs)
                    dve.wait_ge(z_copied, s + 1)
                    cur, prev = zraw[0:rows, s % 2, 0:f, 1:T + 1], zraw[0:rows, s % 2, 0:f, 0:T]
                    diff = shifted[0:rows, 0:f, :]
                    own.did(nc.vector.tensor_tensor(diff, prev, cur, ALU.subtract))
                    own.settle()
                    for j in range(f):
                        ins = nc.vector.scalar_tensor_tensor(out=outs[j], in0=diff[:, j, :],
                                                             scalar=par_("mu", 27)[0:rows, mus[j]:mus[j] + 1],
                                                             in1=cur[:, j, :], op0=ALU.mult, op1=ALU.add)
                    ins.then_inc(z_shifted, 1)
                    dve.wait_ge(z_shifted, s + 1)

                def bc(name):
                    return par_(name).unsqueeze(2).broadcast_to((P, PAIRS, T))

                def op(ins):
                    own.did(ins)
                    own.settle()

                TT, STT = nc.vector.tensor_tensor, nc.vector.scalar_tensor_tensor
                shift(0, [zlora[:, 0, :], zlora[:, 1, :]], [24, 25])
                shift(1, [zlora[0:32, 2, :]], [26], 32)
                dve.wait_ge(lora_act, 3)
                for rows, f0, f1 in ((P, 0, 2), (32, 2, 3)):
                    high = x_high[0:rows, LORA_TILE + f0:LORA_TILE + f1, :]
                    op(nc.vector.tensor_copy(high, zlora[0:rows, f0:f1, :]))
                    ins = TT(x_low[0:rows, LORA_TILE + f0:LORA_TILE + f1, :], zlora[0:rows, f0:f1, :],
                             high.bitcast(F32), ALU.subtract)
                ins.then_inc(lora_low, 1)
                for r in range(4):
                    gb = acc[0] if r % 2 == 0 else acc[3]
                    if r < 3:
                        dve.wait_ge(lora_done, r + 1)
                    else:
                        dve.wait_ge(tiles_used, 2 * START["rkv"])
                    nc.vector.tensor_copy(G8[:, 2 * r:2 * r + 2, :], gb.rearrange("p (f t) -> p f t", f=2))\
                        .then_inc(lora_by_dve, 1)

                def shift_rkv(s):
                    dst, mu = ((K8, KT), (R8, 0), (V8, 2 * KT))[(s - 2) // 4]
                    n = (s - 2) % 4 * 2
                    shift(s, [dst[:, n, :], dst[:, n + 1, :]], [mu + n, mu + n + 1])

                shift_rkv(2)
                dve.wait_ge(lora_by_act, 4)
                C = by_chunk(5)
                for n in range(2 * PAIRS):
                    ins = nc.vector.tensor_tensor_scan(C[:, n, :], ones[:, :], C[:, n, :], 0.0, ALU.mult, ALU.add)
                op(ins)
                nc.vector.tensor_copy(mid, C[:, :, 63])
                op(nc.vector.tensor_copy(startf, C[:, :, 63]))
                midc = mid.rearrange("p (k c) -> p k c", c=2)
                last = C.rearrange("p (k c) t -> p k c t", c=2)[:, :, 0, P - 1]
                op(TT(endf, last, midc[:, :, 0], ALU.subtract))
                op(TT(endf, endf, midc[:, :, 1], ALU.add))
                TT(C, C, mid.unsqueeze(2).broadcast_to((P, 2 * PAIRS, P)), ALU.subtract).then_inc(cum_done, 1)
                for s in range(3, 6):
                    shift_rkv(s)
                TT(KK8, K8, bc("rwkv_k_k"), ALU.mult).then_inc(kk_scaled, 1)
                shift_rkv(6)
                own.did(STT(out=BON, in0=A8, scalar=-1.0, in1=bc("rwkv_k_a"), op0=ALU.add, op1=ALU.mult))
                shift_rkv(7)
                own.settle()
                own.did(STT(out=K8, in0=BON, scalar=1.0, in1=K8, op0=ALU.add, op1=ALU.mult))
                shift_rkv(8)
                dve.wait_ge(kk_root, 1)
                nr = A(6)
                op(nc.vector.tensor_scalar(nr, nr, 1e-12, None, ALU.max))
                op(nc.vector.reciprocal(nr, nr))
                TT(A(3), A(3), nr, ALU.mult).then_inc(kk_done, 1)
                shift_rkv(9)
                op(TT(BON, R8, K8, ALU.mult))
                TT(BON, BON, bc("rwkv_r_k"), ALU.mult).then_inc(rk_done, 1)
                shift_rkv(10)
                dve.wait_ge(kk_done, 1)
                own.did(TT(A(4), A(3), A(4), ALU.mult))
                shift_rkv(11)
                own.settle()
                dve.wait_ge(decays_done, 1)
                TT(A(4), A(4), A(7), ALU.mult)
                TT(A(1), A(1), A(7), ALU.mult).then_inc(bk_decayed, 1)
                shift_rkv(12)
                shift_rkv(13)
                dve.wait_ge(rk_summed, 1)
                TT(A(11), accf, A(2), ALU.mult).then_inc(bonus_done, 1)
                e1, kkc = by_chunk(6), by_chunk(3)
                TT(AR[:, :, 1, :], by_chunk(0), e1, ALU.mult)
                STT(out=AR[:, :, 0, 1:P], in0=kkc[:, :, 1:P], scalar=-1.0, in1=e1[:, :, 0:P - 1], op0=ALU.mult,
                    op1=ALU.mult)
                STT(out=AR[:, :, 0, 0], in0=kkc[:, :, 0], scalar=-1.0, in1=startf, op0=ALU.mult, op1=ALU.mult)\
                    .then_inc(tilde_done, 1)

            def s_rwkv_solve():
                dve.wait_ge(tilde_done, 1)
                dve.wait_ge(turned_vbk, 1)
                up2 = con_("tri_up").unsqueeze(1).broadcast_to((P, 2, 256))
                for g in range(8):
                    for st in (1, 3, 4, 5, 6, 7, 8, 9, 10):
                        if st == 10 and g >= 4:
                            continue
                        for i in range(4):
                            h, c = 4 * (g % 4) + i, g // 4
                            dve.wait_ge(lane_pe[i], 10 * g + st)
                            a, b = wk[i], acc[i]
                            if st == 1:
                                own.did(nc.vector.tensor_tensor(XD[i][:, 0, :], a[:, 0:P], con_("blk_up"), ALU.mult))
                                nc.vector.tensor_tensor(mbk[i].rearrange("p (n t) -> p n t", n=2),
                                                        a.rearrange("p (n t) -> p n t", n=2), up2, ALU.mult)
                                nc.vector.tensor_tensor(XD[i][:, 2, :], b[:, 0:P], con_("blk_low"), ALU.mult)
                                nc.vector.tensor_tensor(LO[i], b[:, 0:P], con_("off_low"), ALU.mult)
                                own.settle()
                                ins = nc.vector.tensor_tensor(XD[i][:, 1, :], XD[i][:, 0, :], ident, ALU.add)
                            elif st in (3, 4, 5):
                                ins = nc.vector.tensor_tensor(XD[i][:, 1, :], XD[i][:, 1, :], b[:, 0:P], ALU.add)
                            elif st == 6:
                                ins = nc.vector.tensor_copy(Ul[i], b[:, 0:64])
                            elif st in (7, 8, 9):
                                ins = nc.vector.tensor_tensor(Ul[i], Ul[i], b[:, 0:64], ALU.add)
                            else:
                                rows = slice(64 * (h % 2), 64 * (h % 2) + 64)
                                ins = nc.vector.tensor_scalar(state[rows, h // 2, :], b[rows, 0:64],
                                                              endf[rows, h // 2:h // 2 + 1], None, ALU.mult)
                            ins.then_inc(lane_dve[i], 1)

            def s_mix_out():
                def op(ins):
                    own.did(ins)
                    own.settle()

                for i in range(4):
                    dve.wait_ge(lane_act[i], lane_counts(7, 10)[1])
                Y = A(6).rearrange("p (h n) -> p h n", n=RW_N)
                shape = (P, 2 * RW_HEADS, RW_N)
                op(nc.vector.tensor_reduce(gsum, Y, AX.X, ALU.add))
                op(nc.vector.tensor_scalar(gsum, gsum, 1.0 / RW_N, None, ALU.mult))
                nc.vector.tensor_tensor(Y, Y, gsum.unsqueeze(2).broadcast_to(shape), ALU.subtract).then_inc(y_centred, 1)
                dve.wait_ge(y_squared, 1)
                nc.vector.tensor_reduce(gvar, A(0).rearrange("p (h n) -> p h n", n=RW_N), AX.X, ALU.add)\
                    .then_inc(y_var, 1)
                dve.wait_ge(y_std, 1)
                op(nc.vector.reciprocal(gvar, gvar))
                nc.vector.tensor_tensor(Y, Y, gvar.unsqueeze(2).broadcast_to(shape), ALU.mult).then_inc(y_normed, 1)
                dve.wait_ge(bias_loaded, 16)

                def biased(n, name, gate):
                    for b in range(4):
                        wait_acc(name, START[name] + 3, b)
                        at = b // 2 * D + b % 2 * 512
                        nc.vector.tensor_tensor(gate[:, at:at + 512], acc[b],
                                                gbias[:, n * D + b % 2 * 512:n * D + b % 2 * 512 + 512], ALU.add)\
                            .then_inc(acc_read, 1)

                biased(0, "gate_a", gate_a)
                dve.wait_ge(y_affine, PAIRS)
                op(nc.vector.tensor_tensor(A(1), A(1), A(11), ALU.add))
                nc.vector.tensor_tensor(A(1), A(1), A(10), ALU.mult).then_inc(z_done, 1)
                biased(1, "gate_r", gate_r)
                for b in range(4):
                    dve.wait_ge(z_high, b + 1)
                    nc.vector.tensor_tensor(x_low[:, 2 * b:2 * b + 2, :].rearrange("p k t -> p (k t)"),
                                            A(1)[:, b * 512:b * 512 + 512], tiles(x_high, 2 * b, 2),
                                            ALU.subtract).then_inc(z_low, 1)
                dve.wait_ge(gate_done, 1)
                for b in range(4):
                    wait_acc("attn_up", START["attn_up"], b)
                    at = b // 2 * D + b % 2 * 512
                    nc.vector.tensor_tensor(merged[:, at:at + 512], acc[b], gate_a[:, at:at + 512], ALU.mult)\
                        .then_inc(acc_read, 1)
                dve.wait_ge(gate_done, 2)
                for tok in range(NT):
                    for b in (2 * tok, 2 * tok + 1):
                        wait_acc("rwkv_out", START["rwkv_out"] + 3, b)
                        at = slice(b * 512, b * 512 + 512)
                        nc.vector.tensor_tensor(mpart[:, at], acc[b], gate_r[:, at], ALU.mult).then_inc(acc_read, 1)
                    dve.wait_ge(acc_read, 4 * ACC["rwkv_out"] + 2 * tok + 2)
                    half = slice(tok * D, tok * D + D)
                    nc.vector.tensor_tensor(merged[:, half], merged[:, half], mpart[:, half], ALU.add)\
                        .then_inc(merge_done, 1)
                for b in range(4):
                    dve.wait_ge(merge_high, b + 1)
                    nc.vector.tensor_tensor(x_low[:, 2 * b:2 * b + 2, :].rearrange("p k t -> p (k t)"), wk[b],
                                            tiles(x_high, 2 * b, 2), ALU.subtract).then_inc(merge_low, 1)
                add_to_x("mix_out", START["mix_out"] + 3, 1.0)

            def s_ffn2():
                norm("ffn2")
                norm_gain("ffn2", [("ffn2_norm", 0)])
                gated_block("ffn2", FFN_GROUPS, 0.5)

            def s_ret():
                norm("mid")
                dve.wait_ge(norm_scaled, NT * (NORM["mid"] + 1))
                dve.wait_ge(gain_loaded, 16)
                nc.vector.tensor_tensor(x[:, :, :], xn, gain_row.unsqueeze(1).broadcast_to((P, NT, D)), ALU.mult)\
                    .then_inc(x_scaled, 1)
                norm("ret")
                norm_gain("ret", [("ret_norm_2", 0)])
                dve.wait_ge(second_tables, 16)
                cs, sn = (con_(n).unsqueeze(1).broadcast_to((P, 2, T)) for n in ("ret_cos", "ret_sin"))
                for m in range(8):
                    dve.wait_ge(tiles_used, 2 * (START["ret_qk"] + m + 1))
                    bank = wk[m % 4].rearrange("p (f t) -> p f t", f=2)
                    q = m % 2
                    c_, s_ = ret_tmp[:, 2 * q], ret_tmp[:, 2 * q + 1]
                    dst = (ret_q if m < 4 else ret_k)[:, m % 4 * 2:m % 4 * 2 + 2, :]
                    nc.vector.tensor_tensor(c_, bank, cs, ALU.mult)
                    nc.vector.tensor_tensor(s_, bank, sn, ALU.mult).then_inc(rot_read, 1)
                    dve.wait_ge(rot_read, m + 1)
                    nc.vector.tensor_tensor(dst[:, 0, :], c_[:, 0, :], s_[:, 1, :], ALU.subtract)
                    nc.vector.tensor_tensor(dst[:, 1, :], s_[:, 0, :], c_[:, 1, :], ALU.add).then_inc(rot_done, 1)
                for n in range(2):
                    for b in range(4):
                        wait_acc(f"ret_v{n}", START["ret_v"] + 4 * n + 3, b)
                        at = n * D + b % 2 * 512
                        nc.vector.tensor_copy(ret_v[:, b // 2, at:at + 512], acc[b]).then_inc(acc_read, 1)
                for h in range(RET_HEADS):
                    dve.wait_ge(rs_ready, h + 1)
                    decay = con_("ret_decay")[:, h * T:h * T + T]
                    nc.vector.tensor_tensor(ret_sT[:, h, 0:T], wk[h][:, 0:T], decay, ALU.mult)
                    nc.vector.tensor_tensor(ret_sT[:, h, T:T + P], wk[h][:, T:T + P], decay[:, 0:P], ALU.mult)\
                        .then_inc(rs_masked, 1)

                def normed(h):
                    dve.wait_ge(o_std, h + 1)
                    dve.wait_ge(acc_read, 4 * ACC["ret_g1"] + 4)
                    own.did(nc.vector.reciprocal(ret_std[:, NT * h:NT * h + NT], ret_std[:, NT * h:NT * h + NT]))
                    own.settle()
                    for tok in range(NT):
                        u = NT * h + tok
                        at = slice(h * RET_DV, (h + 1) * RET_DV)
                        nc.vector.scalar_tensor_tensor(out=ret_y[:, tok, at], in0=acc[2 * (h % 2) + tok],
                                                       scalar=ret_std[:, u:u + 1], in1=ret_g[:, tok, at],
                                                       op0=ALU.mult, op1=ALU.mult).then_inc(ret_y_done, 1)

                def low(h):
                    dve.wait_ge(ret_high, h + 1)
                    nc.vector.tensor_tensor(x_low[:, 4 * h:4 * h + 4, :].rearrange("p k t -> p (k t)"),
                                            wkf[:, 1024 * (h % 2):1024 * (h % 2) + 1024], tiles(x_high, 4 * h, 4),
                                            ALU.subtract).then_inc(ret_low, 1)

                normed(0)
                normed(1)
                for h in range(RET_HEADS):
                    low(h)
                    if h + 2 < RET_HEADS:
                        normed(h + 2)
                add_to_x("ret_out", START["ret_out"] + 7, 1.0)

            def s_moe(l):
                name = f"moe{l}"
                dve.wait_ge(router_high, l + 1)
                nc.vector.tensor_tensor(route_low[:, :], par_(f"route_w{l}", KT * ROUTE), route_high[:, :].bitcast(F32),
                                        ALU.subtract).then_inc(router_low, 1)
                norm(name)
                norm_gain(name, [(f"ffn_norm_{l}", 0)])

                def op(ins):
                    own.did(ins)
                    own.settle()

                def take(at, *shape):
                    flat = scratch[:, at:at + int(np.prod(shape))]
                    names = "abc"[:len(shape)]
                    return flat.rearrange(f"p ({' '.join(names)}) -> p {' '.join(names)}", **dict(zip(names, shape)))

                def wide(t, n):
                    return t.unsqueeze(2).broadcast_to((P, NT, n))

                TT = nc.vector.tensor_tensor
                logits = take(40, NT, ROUTE)
                dve.wait_ge(routed, l + 1)
                op(TT(logits, ps[:, 4:6, 0:ROUTE],
                      par_(f"route_b{l}", ROUTE).unsqueeze(1).broadcast_to((P, NT, ROUTE)), ALU.add))
                prob4, first, score, sel, sel2 = (take(a, NT, 4) for a in (100, 110, 120, 130, 140))
                e1, top, total, w1, val = (scratch[:, a:a + NT] for a in (150, 152, 154, 156, 158))
                oh1, oh2, parts = take(160, NT, 4), take(170, NT, 4), take(180, NT, 4, 4)
                ramp = small[:, 12:16].unsqueeze(1).broadcast_to((P, NT, 4))

                def first_max(src, onehot, best):
                    op(nc.vector.tensor_reduce(best, src, AX.X, ALU.max))
                    op(TT(onehot, src, wide(best, 4), ALU.is_equal))
                    op(TT(score, onehot, ramp, ALU.mult))
                    op(nc.vector.tensor_reduce(total, score, AX.X, ALU.max))
                    op(TT(onehot, score, wide(total, 4), ALU.is_equal))

                op(nc.vector.tensor_reduce(top, logits[:, :, 0:4], AX.X, ALU.max))
                TT(prob4, logits[:, :, 0:4], wide(top, 4), ALU.subtract).then_inc(route_shifted, 1)
                dve.wait_ge(route_exp, l + 1)
                op(nc.vector.tensor_reduce(total, prob4, AX.X, ALU.add))
                op(nc.vector.reciprocal(total, total))
                op(TT(prob4, prob4, wide(total, 4), ALU.mult))
                first_max(prob4, first, val)
                op(TT(parts, logits[:, :, 4:20].rearrange("p t (g e) -> p t g e", g=4),
                      first.unsqueeze(3).broadcast_to((P, NT, 4, 4)), ALU.mult))
                op(nc.vector.tensor_reduce(sel, parts.rearrange("p t g e -> p t e g"), AX.X, ALU.add))
                first_max(sel, oh1, top)
                op(nc.vector.scalar_tensor_tensor(out=sel2, in0=oh1, scalar=MASKED, in1=sel, op0=ALU.mult, op1=ALU.add))
                first_max(sel2, oh2, w1)
                TT(e1, w1, top, ALU.subtract).then_inc(route_diff, 1)
                dve.wait_ge(route_exp2, l + 1)
                op(nc.vector.tensor_scalar(w1, e1, 1.0, None, ALU.add))
                op(nc.vector.reciprocal(w1, w1))
                op(TT(w1, w1, val, ALU.mult))
                op(TT(e1, e1, w1, ALU.mult))
                op(TT(oh1, oh1, wide(w1, 4), ALU.mult))
                op(TT(oh2, oh2, wide(e1, 4), ALU.mult))
                op(TT(oh1, oh1, oh2, ALU.add))
                TT(scratch[:, 0:2 * EXPERTS].rearrange("p (t g e) -> p t g e", t=NT, g=4),
                   first.unsqueeze(3).broadcast_to((P, NT, 4, 4)),
                   oh1.unsqueeze(2).broadcast_to((P, NT, 4, 4)), ALU.mult).then_inc(combine_ready, 1)
                dve.wait_ge(combine_turned, l + 1)
                nc.vector.tensor_copy(weightT[0:EXPERTS, :], acc[2][0:EXPERTS, 0:T]).then_inc(weightT_ready, 1)
                dve.wait_ge(spread_read, 4 * l + 1)
                gated_block(name, MOE_GROUPS, 1.0, GROUP0[name] - GROUP0["moe0"])

            def s_moba():
                norm("moba")
                norm_gain("moba", [("kv_norm_2", 0), ("attn_norm_2", KT)])
                rope("moba_k", 4, moba_k, "moba_cos", "moba_sin")
                for b in range(4):
                    wait_acc("moba_v", START["moba_v"] + 3, b)
                    nc.vector.tensor_copy(moba_v[:, b // 2, b % 2 * 512:b % 2 * 512 + 512], acc[b]).then_inc(acc_read, 1)
                rope("moba_q", 4, moba_q, "moba_cos", "moba_sin")
                attention(moba)
                add_to_x("moba_out", START["moba_out"] + 3, 1.0)

            def s_final():
                norm("final")
                dve.wait_ge(norm_scaled, NT * (NORM["final"] + 1))
                dve.wait_ge(gain_loaded, 32)
                nc.vector.tensor_tensor(final_out, xn, gain_row.unsqueeze(1).broadcast_to((P, NT, D)), ALU.mult)\
                    .then_inc(stored_ready, 1)

            s_ffn1()
            s_dil()
            s_rwkv_in()
            s_rwkv_solve()
            s_mix_out()
            s_ffn2()
            s_ret()
            s_moe(0)
            s_moba()
            s_moe(1)
            s_final()


_OUT = "out_0_dram"


def kernel(**inputs):
    import concourse.bacc as _bacc
    from concourse.bass_utils import run_bass_kernel_spmd as _run

    w = {k: np.asarray(v) for k, v in inputs.items()}
    nc = _bacc.Bacc("TRN2", target_bir_lowering=False, num_devices=1)
    arrays = {
        "in_stream": weight_stream(w), "in_params": param_table(w), "in_consts": const_table(),
        "in_x": np.ascontiguousarray(w["x"][0]), "in_gate_bias": np.ascontiguousarray(w["gate_bias"]),
        "in_gains": np.stack([w["final_norm"], w["final_norm_2"]]),
    }
    aps = [nc.dram_tensor(n, a.shape, F32, kind="ExternalInput").ap() for n, a in arrays.items()]
    aps.append(nc.dram_tensor(_OUT, (T, D), F32, kind="ExternalOutput").ap())
    two_blocks(nc, *aps)
    r = _run(nc, [arrays], core_ids=[0])
    return np.asarray(r.results[0][_OUT]).reshape(1, T, D)
```
